# Optimizing a Trainium2 kernel written in Bass

```python
import jax, jax.numpy as jnp
from jax import lax
import numpy as np

D_MODEL = 2048
BATCH = 1
SEQ = 256
DEPTH = 1

CHUNK = 64
N_HEADS = 32
N_KV_HEADS = 4
HEAD_DIM = 64
WINDOW = 128
WIN_CHUNKS = WINDOW // CHUNK
D_CONV = D_MODEL
CONV_WIDTH = 31
D_FF = 5632
FFN_CONV_WIDTH = 3
EPS = 1e-6
NEG_INF = -1e30
ATTN_W = N_HEADS * HEAD_DIM
KV_W = N_KV_HEADS * HEAD_DIM
D_IN = ATTN_W + 2 * KV_W + 2 * D_CONV + 2 * D_MODEL

kernel_name = "hybrid_swa_sink_conformer_convffn"

def _rms_norm(x, g):
    xf = x.astype(jnp.float32)
    y = xf * lax.rsqrt(jnp.mean(xf * xf, axis=-1, keepdims=True) + EPS)
    return (y * g.astype(jnp.float32)).astype(x.dtype)

def _layer_norm(x, g, b):
    xf = x.astype(jnp.float32)
    mu = jnp.mean(xf, axis=-1, keepdims=True)
    xc = xf - mu
    y = xc * lax.rsqrt(jnp.mean(xc * xc, axis=-1, keepdims=True) + EPS)
    return (y * g.astype(jnp.float32) + b.astype(jnp.float32)).astype(x.dtype)

def _causal_dwconv(x, w):
    k_width, c = w.shape
    return lax.conv_general_dilated(
        x, w[:, None, :].astype(x.dtype), window_strides=(1,), padding=[(k_width - 1, 0)],
        dimension_numbers=('NWC', 'WIO', 'NWC'), feature_group_count=c)

def _band(t, n_chunks):
    b, _, h, dh = t.shape
    tc = t.reshape(b, n_chunks, CHUNK, h, dh)
    tp = jnp.pad(tc, ((0, 0), (WIN_CHUNKS - 1, 0), (0, 0), (0, 0), (0, 0)))
    return jnp.concatenate([tp[:, j:j + n_chunks] for j in range(WIN_CHUNKS)], axis=2)

def _alibi_slopes():
    return 2.0 ** (-8.0 * jnp.arange(1, N_HEADS + 1, dtype=jnp.float32) / N_HEADS)

def _sliding_window_attention(q, k, v, q_g, k_g, sinks):
    b, t, _ = q.shape
    nc = t // CHUNK
    grp = N_HEADS // N_KV_HEADS
    band = WIN_CHUNKS * CHUNK
    qh = _rms_norm(q.reshape(b, t, N_HEADS, HEAD_DIM), q_g).reshape(b, nc, CHUNK, N_KV_HEADS, grp, HEAD_DIM)
    kh = _band(_rms_norm(k.reshape(b, t, N_KV_HEADS, HEAD_DIM), k_g), nc)
    vh = _band(v.reshape(b, t, N_KV_HEADS, HEAD_DIM), nc)
    s = jnp.einsum('bcqhgd,bcshd->bchgqs', qh.astype(jnp.float32), kh.astype(jnp.float32)) * (HEAD_DIM ** -0.5)
    q_pos = (WIN_CHUNKS - 1) * CHUNK + jnp.arange(CHUNK)
    k_pos = jnp.arange(band)
    dist = jnp.abs(q_pos[:, None] - k_pos[None, :]).astype(jnp.float32)
    alibi = (-_alibi_slopes()[:, None, None] * dist).reshape(N_KV_HEADS, grp, CHUNK, band)
    key_chunk = jnp.arange(nc)[:, None] - (WIN_CHUNKS - 1) + k_pos[None, :] // CHUNK
    valid = (key_chunk >= 0)[None, :, None, None, None, :]
    s = jnp.where(valid, s + alibi, NEG_INF)
    sink = jnp.broadcast_to(sinks.astype(jnp.float32).reshape(N_KV_HEADS, grp, 1, 1),
                            (b, nc, N_KV_HEADS, grp, CHUNK, 1))
    p = jax.nn.softmax(jnp.concatenate([s, sink], axis=-1), axis=-1)[..., :band]
    o = jnp.einsum('bchgqs,bcshd->bcqhgd', p.astype(vh.dtype), vh)
    return o.reshape(b, t, ATTN_W)

def _conformer_conv(u, dw_w, dw_b, ln_g, ln_b, w_proj):
    a, gate = jnp.split(u, 2, axis=-1)
    y = a * jax.nn.sigmoid(gate)
    y = _causal_dwconv(y, dw_w) + dw_b
    y = jax.nn.silu(_layer_norm(y, ln_g, ln_b))
    return y @ w_proj

def _conv_ffn(h, w_up, dw_w, w_down):
    u = _causal_dwconv(h @ w_up, dw_w)
    g, val = jnp.split(u, 2, axis=-1)
    return (jax.nn.silu(g) * val) @ w_down

def setup_inputs(seed: int = 0) -> dict:
    key = jax.random.key(seed)
    ks = jax.random.split(key, 16)

    def nrm(k, shape, scale):
        return jax.random.normal(k, shape, jnp.float32) * scale

    L = DEPTH
    return {
        "x": nrm(ks[0], (BATCH, SEQ, D_MODEL), 1.0),
        "norm_mix_g": 1.0 + nrm(ks[1], (L, D_MODEL), 0.02),
        "w_in": nrm(ks[2], (L, D_MODEL, D_IN), D_MODEL ** -0.5),
        "q_norm_g": 1.0 + nrm(ks[3], (L, HEAD_DIM), 0.02),
        "k_norm_g": 1.0 + nrm(ks[4], (L, HEAD_DIM), 0.02),
        "sinks": nrm(ks[5], (L, N_HEADS), 0.5),
        "w_attn_proj": nrm(ks[6], (L, ATTN_W, D_MODEL), ATTN_W ** -0.5),
        "conv_dw_w": nrm(ks[7], (L, CONV_WIDTH, D_CONV), CONV_WIDTH ** -0.5),
        "conv_dw_b": nrm(ks[8], (L, D_CONV), 0.02),
        "conv_ln_g": 1.0 + nrm(ks[9], (L, D_CONV), 0.02),
        "conv_ln_b": nrm(ks[10], (L, D_CONV), 0.02),
        "w_conv_proj": nrm(ks[11], (L, D_CONV, D_MODEL), D_CONV ** -0.5),
        "w_out": nrm(ks[12], (L, D_MODEL, D_MODEL), D_MODEL ** -0.5),
        "norm_ffn_g": 1.0 + nrm(ks[13], (L, D_MODEL), 0.02),
        "w_up": nrm(ks[14], (L, D_MODEL, 2 * D_FF), D_MODEL ** -0.5),
        "ffn_dw_w": nrm(ks[15], (L, FFN_CONV_WIDTH, 2 * D_FF), FFN_CONV_WIDTH ** -0.5),
        "w_down": nrm(jax.random.fold_in(key, 99), (L, D_FF, D_MODEL), D_FF ** -0.5),
    }

def reference(x, norm_mix_g, w_in, q_norm_g, k_norm_g, sinks, w_attn_proj, conv_dw_w, conv_dw_b,
              conv_ln_g, conv_ln_b, w_conv_proj, w_out, norm_ffn_g, w_up, ffn_dw_w, w_down):
    splits = [ATTN_W, ATTN_W + KV_W, ATTN_W + 2 * KV_W, ATTN_W + 2 * KV_W + 2 * D_CONV]
    for l in range(DEPTH):
        n1 = _rms_norm(x, norm_mix_g[l])
        z = n1 @ w_in[l]
        q, k, v, u, gate_logits = jnp.split(z, splits, axis=-1)
        y_a = _sliding_window_attention(q, k, v, q_norm_g[l], k_norm_g[l], sinks[l]) @ w_attn_proj[l]
        y_b = _conformer_conv(u, conv_dw_w[l], conv_dw_b[l], conv_ln_g[l], conv_ln_b[l], w_conv_proj[l])
        g_a, g_b = jnp.split(jax.nn.sigmoid(gate_logits), 2, axis=-1)
        x = x + (g_a * y_a + g_b * y_b) @ w_out[l]
        n2 = _rms_norm(x, norm_ffn_g[l])
        x = x + _conv_ffn(n2, w_up[l], ffn_dw_w[l], w_down[l])
    return x


_drawn_inputs = setup_inputs


def setup_inputs(seed=0):
    import zlib

    import numpy as np

    out = dict(_drawn_inputs(seed))
    spreads = {}
    factors = {'norm_mix_g': 5.811,
     'q_norm_g': 8.0,
     'k_norm_g': 8.0,
     'sinks': 6.976,
     'conv_dw_b': 11.104,
     'conv_ln_g': 22.006,
     'conv_ln_b': 22.256,
     'norm_ffn_g': 10.893}
    for name, (base, spread) in spreads.items():
        noise = np.random.default_rng([zlib.crc32(name.encode()), seed]).standard_normal(out[name].shape)
        drawn = base * np.exp(spread * noise) if base else spread * noise
        out[name] = __import__('jax').numpy.asarray(drawn.astype(out[name].dtype))
    for name, factor in factors.items():
        out[name] = (out[name] * factor).astype(out[name].dtype)
    return out
```

```python
from contextlib import ExitStack, contextmanager

import concourse.bass as bass
from concourse import mybir

ACT = mybir.ActivationFunctionType
ALU = mybir.AluOpType
AX_X = mybir.AxisListType.X
F32 = mybir.dt.float32
F32R = mybir.dt.float32r
ds = bass.ds

P = 128
D = 2048
SEQ = 256
TT = SEQ // P
KT = D // P
COLS = 512
HEADS, KV_HEADS, HD = 32, 4, 64
GROUP = HEADS // KV_HEADS
CHUNK = 64
NCHUNK = SEQ // CHUNK
TAPS = 31
PAD = TAPS - 1
FF = 5632
FT = FF // P
UP_PAIRS = FF // COLS
EPS = 1e-6
KV_W = KV_HEADS * HD

PIECES = 8
PIECE_LEAD = 4
N4 = D // COLS

COL_Q, COL_KV = 0, D
COL_A = D + 2 * KV_W
COL_GLU = COL_A + D
COL_GATE_A = COL_GLU + D
COL_GATE_B = COL_GATE_A + D

Q_U = 0
Q_KV = Q_U + 2 * N4
Q_Q0 = Q_KV + 1
Q_ATT = Q_Q0 + 1
Q_AP = Q_ATT + 2 * N4
Q_CP = Q_AP + 2 * N4 - 1
Q_OUT = Q_CP + N4
Q_UP = Q_OUT + N4
Q_DOWN = Q_UP + 2 * UP_PAIRS
N_DOWN = FT // 4
Q_END = Q_DOWN + N_DOWN

AUX0_NORM1, AUX1_NORM1 = 1, 0
AUX0_GLU = 3
AUX1_KV = 2
AUX0_ATT, AUX1_ATT = AUX0_GLU + N4, AUX1_KV + 1
AUX0_LN, AUX1_LN = AUX0_ATT + 3 * N4, AUX1_ATT + 4 * N4
AUX0_MIX, AUX1_MIX = AUX0_LN + 1, AUX1_LN + 1
AUX0_NORM2, AUX1_NORM2 = AUX0_MIX + 2, AUX1_MIX + 2
AUX0_UP, AUX1_UP = AUX0_NORM2 + 2, AUX1_NORM2 + 2

V_MIX, V_FFN, V_DWB, V_LNG, V_LNB = 0, KT, 2 * KT, 3 * KT, 4 * KT
V_QG = 5 * KT
V_KG = V_QG + 1
NVEC = V_KG + 1


def score_place(n):
    return 2 * (n % 2) + n // 2


class Chain:

    def __init__(self, eng, sem):
        self.eng, self.sem, self.at, self.shift = eng, sem, 0, 0

    def link(self, ins):
        ins.then_inc(self.sem, 1)
        self.at += 1
        self.eng.wait_ge(self.sem, self.at + self.shift)

    @contextmanager
    def loop(self, first, end, per_trip):
        start = self.at
        with self.eng.Fori(first, end) as j:
            self.shift = (j - first) * per_trip
            yield j
        assert self.at - start == per_trip, (self.at - start, per_trip)
        self.at = start + per_trip * (end - first)
        self.shift = 0


def trunk(nc, x, norm_mix_g, w_in, q_norm_g, k_norm_g, sinks, w_attn_proj, conv_dw_w, conv_dw_b,
          conv_ln_g, conv_ln_b, w_conv_proj, w_out, norm_ffn_g, w_up, ffn_dw_w, w_down, out):
    ctx = ExitStack()
    with ctx:
        def sb(name, shape, dt=F32):
            return ctx.enter_context(nc.sbuf_tensor(name, shape, dt))

        def sem(name):
            return ctx.enter_context(nc.semaphore(name))

        raw = sb("raw", [P, PIECE_LEAD, 1024])
        w_hi = sb("w_hi", [P, PIECE_LEAD, 1024], F32R)
        w_lo = sb("w_lo", [P, PIECE_LEAD, 1024], F32R)
        A_hi, A_lo = sb("A_hi", [P, KT, SEQ], F32R), sb("A_lo", [P, KT, SEQ], F32R)
        B_hi, B_lo = sb("B_hi", [P, KT, SEQ], F32R), sb("B_lo", [P, KT, SEQ], F32R)
        xres = sb("xres", [P, TT, D])
        big = sb("big", [P, 2 * TT * D + KT * (PAD + SEQ)])
        gates_a = big[:, 0:TT * D].rearrange("p (t n) -> p t n", t=TT)
        gates_b = big[:, TT * D:2 * TT * D].rearrange("p (t n) -> p t n", t=TT)
        glu = big[:, 2 * TT * D:].rearrange("p (m t) -> p m t", m=KT)
        ff = big[:, 0:FT * SEQ].rearrange("p (m t) -> p m t", m=FT)
        flat = xres[:, :, :].rearrange("p t n -> p (t n)")
        stage1 = flat[:, 0:1024].rearrange("p (t n) -> p t n", t=TT)
        stage2 = flat[:, 1024:2048].rearrange("p (t n) -> p t n", t=TT)
        stage3 = flat[:, 2048:3072].rearrange("p (t n) -> p t n", t=TT)
        q_t = flat[:, 2048:3072].rearrange("p (m t) -> p m t", m=4)
        prob0 = flat[:, 3072:4096]
        squares = flat.rearrange("p (m t) -> p m t", m=KT)
        work1 = sb("work1", [P, 1024])
        work2 = sb("work2", [P, 1024])
        work3 = sb("work3", [P, 1024])
        prob1 = work1[:, :]
        prob_t = work2[:, :]
        v_band = work3[:, :].rearrange("p (c n) -> p c n", c=NCHUNK)
        xn = [work1[:, :].rearrange("p (t n) -> p t n", t=TT), work2[:, :].rearrange("p (t n) -> p t n", t=TT)]
        mix_n = xn[0]
        up_n = xn[0]
        g_t = work2[:, :].rearrange("p (m t) -> p m t", m=4)
        val_t = work3[:, :].rearrange("p (m t) -> p m t", m=4)
        k_t = sb("k_t", [P, KV_HEADS, CHUNK + SEQ])
        k_head = sb("k_head", [P, CHUNK + SEQ])
        v_head = sb("v_head", [P, NCHUNK, HD])
        dist = sb("dist", [P, TT, P])
        dist_raw = sb("dist_raw", [P, TT * P])
        conv_acc = sb("conv_acc", [P, 2, SEQ])
        dw_t = sb("dw_t", [P, KT, TAPS])
        vecs = sb("vecs", [P, NVEC])
        q_gain = sb("q_gain", [P, 1])
        ffn_dw = sb("ffn_dw", [P, 3, 2 * FT])
        neg_slope = sb("neg_slope", [P, HEADS])
        sink_rows = sb("sink_rows", [P, HEADS])
        sink = sb("sink", [P, HEADS])
        ident = sb("ident", [P, P])
        mean_of = sb("mean_of", [P, P])
        stats = sb("stats", [P, 96])
        ssq, rms_ms, rms_sd, rms_r = (stats[:, 2 * n:2 * n + 2] for n in range(4))
        hs_sum, hs_ms, hs_sd, hs_r = (stats[:, 8 + 16 * n:24 + 16 * n] for n in range(4))
        soft = sb("soft", [P, 2, 6, 8])

        ps = ctx.enter_context(nc.psum_tensor("ps", [P, 8, COLS], F32))

        def acc(par):
            return ps[:, 2 * par:2 * par + 2, :]

        def aux(b):
            return ps[:, 4 + 2 * b:6 + 2 * b, :]

        def aux_tiles(b, m=4):
            return aux(b).rearrange("p b n -> p (b n)").rearrange("p (m t) -> p m t", m=m)

        rows_dw = big[0:TAPS, 0:D]
        rows_vec = big[0:NVEC, D:D + P]
        rows_ffn = big[0:2 * FT, D + P:D + 4 * P].rearrange("p (k n) -> p k n", k=3)
        junk = gates_b

        raw_landed = [sem(f"raw_landed{i}") for i in range(PIECE_LEAD)]
        hi_ready, lo_ready, piece_used = sem("hi_ready"), sem("lo_ready"), sem("piece_used")
        evacuated = [sem("evacuated_even"), sem("evacuated_odd")]
        aux_written = [sem("aux_written0"), sem("aux_written1")]
        aux_drained = [sem("aux_drained0"), sem("aux_drained1")]
        x_landed, params_landed = sem("x_landed"), sem("params_landed")
        x_reloaded = sem("x_reloaded")
        consts_ready, iota_ready, consts_done = sem("consts_ready"), sem("iota_ready"), sem("consts_done")
        pool_step = sem("pool_step")
        dve_step = sem("dve_step")
        ssq_ready, ms_ready, sd_ready, xn_ready, norm_hi = (sem(n) for n in (
            "ssq_ready", "ms_ready", "sd_ready", "xn_ready", "norm_hi"))
        glu_ready = sem("glu_ready")
        k_ready, v_shifted = sem("k_ready"), sem("v_shifted")
        hs_ms_ready, hs_sd_ready, qn_ready = (sem(n) for n in ("hs_ms_ready", "hs_sd_ready", "qn_ready"))
        max_ready, exp_ready, prob_ready, o_hi_ready = (sem(n) for n in (
            "max_ready", "exp_ready", "prob_ready", "o_hi_ready"))
        conv_tap = sem("conv_tap")
        centred, squared, var_sd, ln_scaled, ln_silu, conv_hi, conv_lo = (sem(n) for n in (
            "centred", "squared", "var_sd", "ln_scaled", "ln_silu", "conv_hi", "conv_lo"))
        mix_ready, mix_hi = sem("mix_ready"), sem("mix_hi")
        g_silu, ff_ready = sem("g_silu"), sem("ff_ready")
        ff_hi_ready, ff_lo_ready = sem("ff_hi_ready"), sem("ff_lo_ready")
        bank_done, y_ready, stored = sem("bank_done"), sem("y_ready"), sem("stored")

        block = ctx.enter_context(nc.Block())

        def left_psum(eng, c, j=0):
            eng.wait_ge(evacuated[c % 2], j + (c // 2 + 1))

        @block.sync
        def _(sp):
            sp.dma_start(xres[:], x[0].rearrange("(t p) n -> p t n", p=P)).then_inc(x_landed, 16)

            def load_chunk(q, w, c0, first=0):
                rows = w.rearrange("(i r p) n -> i p r n", r=2, p=P)
                for i in range(PIECES):
                    if i >= first:
                        sp.wait_ge(lo_ready, q * PIECES + i - (PIECE_LEAD - 1))
                    sp.dma_start(raw[:, i % PIECE_LEAD, :].rearrange("p (r n) -> p r n", r=2),
                                 rows[i][:, :, ds(c0, COLS)]).then_inc(raw_landed[i % PIECE_LEAD], 16)

            wi = w_in[0]
            load_chunk(Q_U, wi, COL_A, first=PIECE_LEAD)
            with sp.Fori(0, N4 - 1) as j:
                load_chunk(Q_U + 1 + j * 2, wi, COL_GLU + j * COLS)
                load_chunk(Q_U + 2 + j * 2, wi, COL_A + COLS + j * COLS)
            load_chunk(Q_KV - 1, wi, COL_GLU + (N4 - 1) * COLS)
            load_chunk(Q_KV, wi, COL_KV)
            load_chunk(Q_Q0, wi, COL_Q)
            with sp.Fori(0, N4 - 1) as j:
                load_chunk(Q_ATT + j * 2, wi, COL_GATE_A + j * COLS)
                load_chunk(Q_ATT + 1 + j * 2, wi, COL_Q + COLS + j * COLS)
            load_chunk(Q_AP - 2, wi, COL_GATE_A + (N4 - 1) * COLS)
            load_chunk(Q_AP - 1, wi, COL_GATE_B)
            with sp.Fori(0, N4 - 1) as j:
                load_chunk(Q_AP + j * 2, w_attn_proj[0], j * COLS)
                load_chunk(Q_AP + 1 + j * 2, wi, COL_GATE_B + COLS + j * COLS)
            load_chunk(Q_CP - 1, w_attn_proj[0], (N4 - 1) * COLS)
            with sp.Fori(0, N4) as j:
                load_chunk(Q_CP + j, w_conv_proj[0], j * COLS)
            sp.wait_ge(aux_written[1], AUX1_LN + 1)
            sp.dma_start(xres[:], x[0].rearrange("(t p) n -> p t n", p=P)).then_inc(x_reloaded, 16)
            with sp.Fori(0, N4) as j:
                load_chunk(Q_OUT + j, w_out[0], j * COLS)
            with sp.Fori(0, UP_PAIRS) as j:
                load_chunk(Q_UP + j * 2, w_up[0], j * COLS)
                load_chunk(Q_UP + 1 + j * 2, w_up[0], FF + j * COLS)
            down_rows = w_down[0].rearrange("(k p) n -> p k n", p=P)
            with sp.Fori(0, N_DOWN) as it:
                for i in range(PIECES):
                    sp.wait_ge(lo_ready, (Q_DOWN + it) * PIECES + i - (PIECE_LEAD - 1))
                    half = i % 2
                    sp.dma_start(raw[:, i % PIECE_LEAD:i % PIECE_LEAD + 1, :],
                                 down_rows[:, ds(it * 4 + i // 2, 1), half * 1024:(half + 1) * 1024]
                                 ).then_inc(raw_landed[i % PIECE_LEAD], 16)
            dst = out[0].rearrange("(t p) n -> p t n", p=P)
            for n in range(N4):
                for t in range(TT):
                    sp.wait_ge(y_ready, n * TT + t + 1)
                    sp.dma_start(dst[:, t, n * COLS:(n + 1) * COLS],
                                 xres[:, t, n * COLS:(n + 1) * COLS]).then_inc(stored, 16)
            sp.wait_ge(stored, 16 * N4 * TT)

        @block.gpsimd
        def _(pool):
            n = 0

            def step(ins):
                nonlocal n
                ins.then_inc(pool_step, 1)
                n += 1
                pool.wait_ge(pool_step, n)

            step(nc.gpsimd.memset(ident[:], 0.0))
            nc.gpsimd.affine_select(out=ident[:], in_=ident[:], compare_op=ALU.not_equal, fill=1.0, base=0,
                                    pattern=[[-1, P]], channel_multiplier=1).then_inc(consts_ready, 1)
            pool.wait_ge(consts_ready, 1)
            for half in range(2):
                nc.gpsimd.iota(dist_raw[64 * half:64 * half + 64, :].rearrange("p (t s) -> p t s", t=TT),
                               pattern=[[0, TT], [-1, P]], base=CHUNK, channel_multiplier=1,
                               allow_small_or_imprecise_dtypes=True).then_inc(iota_ready, 1)
                pool.wait_ge(iota_ready, half + 1)
            step(nc.gpsimd.memset(mean_of[:], 1.0 / D))
            for h in range(HEADS):
                at = h // 4 * 4 + score_place(h % 4)
                step(nc.gpsimd.memset(neg_slope[:, at:at + 1], -(2.0 ** (-8.0 * (h + 1) / HEADS))))
            nc.gpsimd.memset(k_t[:, :, 0:CHUNK], 0.0).then_inc(consts_done, 1)

        @block.scalar
        def _(act):
            def split_hi(q, i):
                s = i % PIECE_LEAD
                act.wait_ge(raw_landed[s], (q * 2 + 2 + i // PIECE_LEAD) * 16)
                act.wait_ge(piece_used, q * PIECES + i + 1)
                nc.scalar.activation(w_hi[:, s, :], raw[:, s, :], ACT.Copy).then_inc(hi_ready, 1)

            def chunk(q, hooks={}):
                for i in range(PIECES):
                    if i in hooks:
                        hooks[i]()
                    split_hi(q, i)

            def finished(q):
                act.wait_ge(piece_used, (q + 1) * PIECES)

            def norm(first_stat, aux_base, stat_hi, gain_col):
                for t in range(TT):
                    nc.scalar.activation(junk[:, t, :], xres[:, t, :], ACT.Square,
                                         accum_out=ssq[:, t:t + 1]).then_inc(ssq_ready, 1)
                act.wait_ge(ms_ready, first_stat + 1)
                nc.scalar.activation(rms_sd, rms_ms, ACT.Sqrt).then_inc(sd_ready, 1)
                for c in range(4):
                    act.wait_ge(aux_written[c % 2], aux_base[c % 2] + c // 2 + 1)
                    for m in range(4):
                        k = 4 * c + m
                        nc.scalar.activation(stat_hi[:, k, :], aux_tiles(c % 2)[:, m, :], ACT.Copy,
                                             scale=vecs[:, gain_col + k:gain_col + k + 1]).then_inc(norm_hi, 1)

            act.dma_start(rows_vec[0:KT, :], norm_mix_g[0].rearrange("(m n) -> m n", n=P)).then_inc(params_landed, 16)
            for n, v in enumerate((norm_ffn_g, conv_dw_b, conv_ln_g, conv_ln_b)):
                act.dma_start(rows_vec[(n + 1) * KT:(n + 2) * KT, :],
                              v[0].rearrange("(m n) -> m n", n=P)).then_inc(params_landed, 16)
            for n, v in enumerate((q_norm_g, k_norm_g)):
                for half in range(2):
                    act.dma_start(rows_vec[V_QG + n:V_QG + n + 1, half * HD:(half + 1) * HD],
                                  v).then_inc(params_landed, 16)
            act.dma_start(rows_dw, conv_dw_w[0]).then_inc(params_landed, 16)
            act.dma_start(rows_ffn, ffn_dw_w[0].rearrange("k (m n) -> m k n", n=P)).then_inc(params_landed, 16)
            act.dma_start(sink_rows[:], sinks.partition_broadcast(P)).then_inc(params_landed, 16)

            act.wait_ge(x_landed, 16)
            for i in range(PIECE_LEAD):
                act.wait_ge(raw_landed[i], 16)
                nc.scalar.activation(w_hi[:, i, :], raw[:, i, :], ACT.Copy).then_inc(hi_ready, 1)
            act.wait_ge(aux_drained[0], 1)
            norm(0, (AUX0_NORM1, AUX1_NORM1), A_hi, V_MIX)

            def glu_out(j):
                act.wait_ge(aux_written[0], AUX0_GLU + 1 + j)
                nc.scalar.activation(glu[:, ds(j * 4, 4), PAD:], aux_tiles(0), ACT.Copy).then_inc(aux_drained[0], 1)

            def evac(c, j, dst, func):
                finished(c + j * 2)
                nc.scalar.activation(dst, acc(c % 2), func).then_inc(evacuated[c % 2], 1)

            chunk(Q_U)
            evac(Q_U, 0, stage1, ACT.Copy)
            with act.Fori(0, N4 - 1) as j:
                chunk(Q_U + 1 + j * 2)
                evac(Q_U + 1, j, stage3, ACT.Sigmoid)
                chunk(Q_U + 2 + j * 2, {3: lambda: glu_out(j)})
                evac(Q_U + 2, j, stage1, ACT.Copy)
            chunk(Q_KV - 1)
            evac(Q_KV - 1, 0, stage3, ACT.Sigmoid)
            chunk(Q_KV, {3: lambda: glu_out(N4 - 1)})
            evac(Q_KV, 0, stage1, ACT.Copy)

            left_psum(act, Q_KV)
            act.dma_start(v_band[64:P, 0, :], stage1[0:64, 0, KV_W:]).then_inc(v_shifted, 16)
            act.dma_start(v_band[0:64, 2, :], stage1[64:P, 0, KV_W:]).then_inc(v_shifted, 16)
            act.dma_start(v_band[64:P, 2, :], stage1[0:64, 1, KV_W:]).then_inc(v_shifted, 16)

            def head_root(n):
                act.wait_ge(hs_ms_ready, n + 1)
                nc.scalar.activation(hs_sd, hs_ms, ACT.Sqrt).then_inc(hs_sd_ready, 1)

            def k_out():
                act.wait_ge(aux_written[1], AUX1_KV + 1)
                nc.scalar.activation(k_t[:, :, CHUNK:], aux_tiles(1), ACT.Copy,
                                     scale=vecs[:, V_KG:V_KG + 1]).then_inc(aux_drained[1], 1)
                act.wait_ge(v_shifted, 48)

            chunk(Q_Q0, {1: lambda: head_root(0), 3: k_out})
            evac(Q_Q0, 0, stage1, ACT.Copy)

            def q_out(j):
                act.wait_ge(aux_written[1], AUX1_ATT + 1 + j * 4)
                nc.scalar.activation(q_t, aux_tiles(1), ACT.Copy, scale=q_gain[:]).then_inc(aux_drained[1], 1)

            def exps(j, e):
                act.wait_ge(max_ready, j * 2 + e + 1)
                p = (prob0, prob1)[e]
                s = soft[:, e]
                for n in range(8):
                    nc.scalar.activation(p[:, n * P:(n + 1) * P], p[:, n * P:(n + 1) * P], ACT.Exp,
                                         bias=s[:, 1, n:n + 1], accum_out=s[:, 3, n:n + 1])
                nc.scalar.activation(s[:, 4, :], s[:, 2, :], ACT.Exp).then_inc(exp_ready, 1)

            def prob_out(j, e):
                act.wait_ge(aux_written[0], AUX0_ATT + 2 + e + j * 3)
                nc.scalar.activation(prob_t, aux(0).rearrange("p b n -> p (b n)"), ACT.Copy).then_inc(aux_drained[0], 1)

            def o_out(j, e):
                act.wait_ge(aux_written[1], AUX1_ATT + 3 + e + j * 4)
                nc.scalar.activation(B_hi[:, ds(j * 4 + 2 * e, 2), :], aux_tiles(1)[:, 0:2, :],
                                     ACT.Copy).then_inc(o_hi_ready, 1)

            def att_hooks(j):
                return ({1: lambda: head_root(j + 1), 3: lambda: q_out(j), 5: lambda: exps(j, 0),
                         7: lambda: prob_out(j, 0)},
                        {0: lambda: o_out(j, 0), 1: lambda: exps(j, 1), 4: lambda: prob_out(j, 1),
                         6: lambda: o_out(j, 1)})

            with act.Fori(0, N4 - 1) as j:
                first, second = att_hooks(j)
                chunk(Q_ATT + j * 2, first)
                evac(Q_ATT, j, gates_a[:, :, ds(j * COLS, COLS)], ACT.Sigmoid)
                chunk(Q_ATT + 1 + j * 2, second)
                evac(Q_ATT + 1, j, stage1, ACT.Copy)
            first, second = att_hooks(N4 - 1)
            chunk(Q_AP - 2, first)
            evac(Q_AP - 2, 0, gates_a[:, :, (N4 - 1) * COLS:], ACT.Sigmoid)
            chunk(Q_AP - 1, second)
            evac(Q_AP - 1, 0, gates_b[:, :, 0:COLS], ACT.Sigmoid)

            with act.Fori(0, N4 - 1) as j:
                chunk(Q_AP + j * 2)
                chunk(Q_AP + 1 + j * 2)
                evac(Q_AP + 1, j, gates_b[:, :, ds(COLS + j * COLS, COLS)], ACT.Sigmoid)
            chunk(Q_CP - 1)

            for c in range(4):
                if c < 3:
                    act.wait_ge(centred, c + 1)
                else:
                    act.wait_ge(aux_drained[0], AUX0_LN + 1)
                nc.scalar.activation(squares[:, 4 * c:4 * c + 4, :], glu[:, 4 * c:4 * c + 4, PAD:],
                                     ACT.Square).then_inc(squared, 1)
            act.wait_ge(aux_drained[1], AUX1_LN + 1)
            nc.scalar.activation(conv_acc[:, 1, :], conv_acc[:, 0, :], ACT.Sqrt).then_inc(var_sd, 1)
            for c in range(4):
                act.wait_ge(ln_scaled, c + 1)
                for m in range(4 * c, 4 * c + 4):
                    last = nc.scalar.activation(glu[:, m, PAD:], glu[:, m, PAD:], ACT.Silu,
                                                scale=vecs[:, V_LNG + m:V_LNG + m + 1],
                                                bias=vecs[:, V_LNB + m:V_LNB + m + 1])
                last.then_inc(ln_silu, 1)
                act.wait_ge(ln_silu, c + 1)
                nc.scalar.activation(A_hi[:, 4 * c:4 * c + 4, :], glu[:, 4 * c:4 * c + 4, PAD:],
                                     ACT.Copy).then_inc(conv_hi, 1)

            def mix_out(c):
                act.wait_ge(aux_written[c % 2], (AUX0_MIX, AUX1_MIX)[c % 2] + c // 2 + 1)
                nc.scalar.activation(B_hi[:, 4 * c:4 * c + 4, :], aux_tiles(c % 2), ACT.Copy).then_inc(mix_hi, 1)

            for c in range(N4):
                chunk(Q_CP + c, {3: lambda: mix_out(c - 1)} if c else {})
            chunk(Q_OUT, {2: lambda: mix_out(N4 - 1)})
            for c in range(1, N4):
                chunk(Q_OUT + c)
            for c in (Q_UP - 2, Q_UP - 1):
                left_psum(act, c)
            norm(1, (AUX0_NORM2, AUX1_NORM2), A_hi, V_FFN)

            def silu_g(j):
                act.wait_ge(aux_drained[0], j + AUX0_UP + 1)
                nc.scalar.activation(g_t, g_t, ACT.Silu).then_inc(g_silu, 1)

            chunk(Q_UP)
            evac(Q_UP, 0, up_n, ACT.Copy)
            with act.Fori(0, UP_PAIRS - 1) as j:
                chunk(Q_UP + 1 + j * 2, {6: lambda: silu_g(j)})
                evac(Q_UP + 1, j, up_n, ACT.Copy)
                chunk(Q_UP + 2 + j * 2)
                evac(Q_UP + 2, j, up_n, ACT.Copy)

            def split_ff(kt, s):
                nc.scalar.activation(B_hi[:, s:s + 1, :], ff[:, ds(kt, 1), :], ACT.Copy).then_inc(ff_hi_ready, 1)

            chunk(Q_DOWN - 1, {6: lambda: silu_g(UP_PAIRS - 1)})
            evac(Q_DOWN - 1, 0, up_n, ACT.Copy)
            act.wait_ge(ff_ready, 1)
            split_ff(0, 0)
            split_ff(1, 1)
            act.wait_ge(ff_ready, UP_PAIRS)
            with act.Fori(0, N_DOWN - 1) as it:
                for i in range(PIECES):
                    split_hi(Q_DOWN + it, i)
                    if i % 2 == 0:
                        split_ff(it * 4 + 2 + i // 2, (2 + i // 2) % 4)
            for i in range(PIECE_LEAD):
                split_hi(Q_END - 1, i)
                if i % 2 == 0:
                    split_ff(FT - 2 + i // 2, 2 + i // 2)

        @block.vector
        def _(dve):
            links = Chain(dve, dve_step)
            link = links.link

            def split_lo(q, i):
                s = i % PIECE_LEAD
                dve.wait_ge(hi_ready, q * PIECES + PIECE_LEAD + i + 1)
                nc.vector.tensor_tensor(w_lo[:, s, :], raw[:, s, :], w_hi[:, s, :].bitcast(F32),
                                        ALU.subtract).then_inc(lo_ready, 1)

            def chunk(q, hooks={}, taps_of=None, taps=None):
                for i in range(PIECES):
                    if i in hooks:
                        hooks[i]()
                    split_lo(q, i)
                    if taps_of is not None:
                        n = (taps[1] - taps[0]) // PIECES
                        conv_taps(taps_of, taps[0] + i * n, taps[0] + (i + 1) * n)

            def conv_taps(m, k0, k1):
                tile = glu[:, ds(m, 1), :].rearrange("p m t -> p (m t)")
                for k in range(k0, k1):
                    a = conv_acc[:, k % 2, :]
                    if k >= 1:
                        dve.wait_ge(conv_tap, m * 32 + (k if k in (1, 30, 31) else k - 1))
                    if k < 31:
                        src = tile[:, k:k + SEQ]
                        w = dw_t[:, ds(m, 1), k:k + 1].rearrange("p m k -> p (m k)")
                    if k == 0:
                        bias = vecs[:, ds(m + V_DWB, 1)]
                        ins = nc.vector.tensor_scalar(a, src, w, bias, ALU.mult, ALU.add)
                    elif k == 1:
                        ins = nc.vector.tensor_scalar(a, src, w, None, ALU.mult)
                    elif k < 30:
                        ins = nc.vector.scalar_tensor_tensor(out=a, in0=src, scalar=w, in1=a,
                                                             op0=ALU.mult, op1=ALU.add)
                    elif k == 30:
                        ins = nc.vector.scalar_tensor_tensor(out=tile[:, PAD:], in0=src, scalar=w, in1=a,
                                                             op0=ALU.mult, op1=ALU.add)
                    else:
                        ins = nc.vector.tensor_tensor(tile[:, PAD:], tile[:, PAD:], a, ALU.add)
                    ins.then_inc(conv_tap, 1)

            def norm(first_stat, aux_base, stat_hi, stat_lo, gain_col):
                dve.wait_ge(ssq_ready, 2 * first_stat + 2)
                nc.vector.tensor_scalar(rms_ms, ssq, 1.0 / D, EPS, ALU.mult, ALU.add).then_inc(ms_ready, 1)
                dve.wait_ge(sd_ready, first_stat + 1)
                link(nc.vector.reciprocal(rms_r, rms_sd))

                def scale_rows(c):
                    for t in range(TT):
                        nc.vector.tensor_scalar(xn[c % 2][:, t, :], xres[:, t, c * COLS:(c + 1) * COLS],
                                                rms_r[:, t:t + 1], None, ALU.mult).then_inc(xn_ready, 1)

                def lo_rows(c):
                    for m in range(4):
                        k = 4 * c + m
                        if m % 2 == 0:
                            dve.wait_ge(norm_hi, 16 * first_stat + k + 2)
                        last = nc.vector.scalar_tensor_tensor(
                            out=stat_lo[:, k, :], in0=aux_tiles(c % 2)[:, m, :],
                            scalar=vecs[:, gain_col + k:gain_col + k + 1], in1=stat_hi[:, k, :].bitcast(F32),
                            op0=ALU.mult, op1=ALU.subtract)
                    last.then_inc(aux_drained[c % 2], 1)

                scale_rows(0)
                scale_rows(1)
                for c in range(4):
                    lo_rows(c)
                    if c + 2 < 4:
                        scale_rows(c + 2)

            link(nc.vector.memset(glu[:, :, 0:PAD], 0.0))
            nc.vector.memset(v_band[0:64, 0, :], 0.0)
            dve.wait_ge(iota_ready, 2)
            link(nc.vector.scalar_tensor_tensor(out=dist[:, :, :].rearrange("p t s -> p (t s)"), in0=dist_raw[:],
                                                scalar=-1.0, in1=dist_raw[:], op0=ALU.mult, op1=ALU.max))
            link(nc.vector.memset(dist[0:CHUNK, 0, 0:CHUNK], 1e30))
            dve.wait_ge(params_landed, 12 * 16)
            nc.vector.tensor_copy(sink[:].rearrange("p (g b a) -> p g b a", a=2, b=2),
                                  sink_rows[:].rearrange("p (g a b) -> p g b a", a=2, b=2))
            dve.wait_ge(aux_written[0], 1)
            nc.vector.tensor_copy(dw_t[:], ps[:, 4, :].rearrange("p (m k) -> p m k", k=32)[:, :, 0:TAPS])
            link(nc.vector.tensor_copy(vecs[:], ps[:, 5, 0:NVEC]))
            nc.vector.tensor_scalar(q_gain[:], vecs[:, V_QG:V_QG + 1], HD ** -0.5, None, ALU.mult)
            nc.vector.tensor_copy(ffn_dw[:], ps[:, 5, P:P + 6 * FT].rearrange("p (k m) -> p k m", k=3)
                                  ).then_inc(aux_drained[0], 1)
            for i in range(PIECE_LEAD):
                dve.wait_ge(hi_ready, i + 1)
                nc.vector.tensor_tensor(w_lo[:, i, :], raw[:, i, :], w_hi[:, i, :].bitcast(F32),
                                        ALU.subtract).then_inc(lo_ready, 1)
            norm(0, (AUX0_NORM1, AUX1_NORM1), A_hi, A_lo, V_MIX)

            def glu_product(j):
                left_psum(dve, Q_U + 1, j)
                nc.vector.tensor_tensor(stage2, stage1, stage3, ALU.mult).then_inc(glu_ready, 1)

            def glu_landed(m):
                dve.wait_ge(aux_drained[0], AUX0_GLU + 1 + m // 4)

            chunk(Q_U)
            chunk(Q_U + 1)
            chunk(Q_U + 2, {0: lambda: glu_product(0)})
            with dve.Fori(1, N4 - 1) as j:
                chunk(Q_U + 1 + j * 2, {0: lambda: dve.wait_ge(aux_drained[0], AUX0_GLU + 1)}, j - 1, (0, 32))
                chunk(Q_U + 2 + j * 2, {0: lambda: glu_product(j)})
            chunk(Q_KV - 1, {}, 2, (0, 32))
            chunk(Q_KV, {0: lambda: glu_product(N4 - 1)}, 3, (0, 32))

            def head_rms(src, n_heads, n):
                w = n_heads * HD
                link(nc.vector.tensor_tensor(stage3[:, :, 0:w], src, src, ALU.mult))
                for t in range(TT):
                    last = nc.vector.tensor_reduce(
                        hs_sum[:, t * n_heads:(t + 1) * n_heads],
                        stage3[:, t, 0:w].rearrange("p (h d) -> p h d", d=HD), AX_X, ALU.add)
                link(last)
                nh = TT * n_heads
                if nh < 16:
                    link(nc.vector.memset(hs_sum[:, nh:16], 1.0))
                nc.vector.tensor_scalar(hs_ms, hs_sum, 1.0 / HD, EPS, ALU.mult, ALU.add).then_inc(hs_ms_ready, 1)

            def head_inverse(n):
                dve.wait_ge(hs_sd_ready, n + 1)
                link(nc.vector.reciprocal(hs_r, hs_sd))

            def heads_of(r, t, n_heads):
                return r[:, t * n_heads:(t + 1) * n_heads].unsqueeze(2).to_broadcast([P, n_heads, HD])

            def k_start():
                dve.wait_ge(consts_done, 1)
                left_psum(dve, Q_KV)
                dve.wait_ge(aux_drained[0], AUX0_GLU + N4)
                for t in range(TT):
                    nc.vector.tensor_copy(v_band[:, 2 * t + 1, :], stage1[:, t, KV_W:])
                head_rms(stage1[:, :, 0:KV_W], KV_HEADS, 0)

            def k_rows():
                head_inverse(0)
                for t in range(TT):
                    for dup in range(2):
                        dst = stage2[:, t, :].rearrange("p (g u d) -> p g u d", u=2, d=HD)[:, :, dup, :]
                        last = nc.vector.tensor_tensor(dst, stage1[:, t, 0:KV_W].rearrange("p (g d) -> p g d", d=HD),
                                                       heads_of(hs_r, t, KV_HEADS), ALU.mult)
                last.then_inc(k_ready, 1)

            chunk(Q_Q0, {0: k_start, 2: k_rows}, 4, (0, 32))

            def q_start(j):
                left_psum(dve, Q_Q0, j)
                head_rms(stage1, GROUP, j + 1)

            def q_rows(j):
                head_inverse(j + 1)
                nc.vector.tensor_copy(v_head[:], v_band[:, :, ds(j * HD, HD)])
                nc.vector.tensor_copy(k_head[:], k_t[:, ds(j, 1), :].rearrange("p g t -> p (g t)"))
                for t in range(TT):
                    last = nc.vector.tensor_tensor(
                        stage2[:, t, :].rearrange("p (h d) -> p h d", d=HD),
                        stage1[:, t, :].rearrange("p (h d) -> p h d", d=HD), heads_of(hs_r, t, GROUP), ALU.mult)
                last.then_inc(qn_ready, 1)

            def maxima(j, e):
                b = e
                dve.wait_ge(aux_written[b], (AUX0_ATT + 1 + j * 3, AUX1_ATT + 2 + j * 4)[e])
                p = (prob0, prob1)[e]
                s = soft[:, e]
                for n in range(4):
                    last = nc.vector.scalar_tensor_tensor(
                        out=p[:, n * 256:(n + 1) * 256], in0=dist[:, :, :].rearrange("p t s -> p (t s)"),
                        scalar=neg_slope[:, ds(j * GROUP + 4 * e + n, 1)],
                        in1=aux(b).rearrange("p b n -> p (b n)")[:, n * 256:(n + 1) * 256],
                        op0=ALU.mult, op1=ALU.add)
                last.then_inc(aux_drained[b], 1)
                dve.wait_ge(aux_drained[b], (AUX0_ATT + 1 + j * 3, AUX1_ATT + 2 + j * 4)[e])
                link(nc.vector.tensor_reduce(s[:, 0, :], p.rearrange("p (n s) -> p n s", s=P), AX_X, ALU.max))
                sk = sink[:, ds(j * GROUP + 4 * e, 4)].unsqueeze(2).to_broadcast([P, 4, TT])
                m = s[:, 0, :].rearrange("p (n t) -> p n t", t=TT)
                link(nc.vector.tensor_tensor(m, m, sk, ALU.max))
                nc.vector.tensor_scalar(s[:, 1, :], s[:, 0, :], -1.0, None, ALU.mult)
                nc.vector.tensor_tensor(s[:, 2, :].rearrange("p (n t) -> p n t", t=TT), sk, m,
                                        ALU.subtract).then_inc(max_ready, 1)

            def probs(j, e):
                dve.wait_ge(exp_ready, j * 2 + e + 1)
                p = (prob0, prob1)[e].rearrange("p (n s) -> p n s", s=P)
                s = soft[:, e]
                link(nc.vector.tensor_tensor(s[:, 5, :], s[:, 3, :], s[:, 4, :], ALU.add))
                link(nc.vector.reciprocal(s[:, 0, :], s[:, 5, :]))
                nc.vector.tensor_tensor(p, p, s[:, 0, :].unsqueeze(2).to_broadcast([P, 8, P]),
                                        ALU.mult).then_inc(prob_ready, 1)

            def o_lo(j, e):
                dve.wait_ge(o_hi_ready, j * 2 + e + 1)
                at = ds(j * 4 + 2 * e, 2)
                nc.vector.tensor_tensor(B_lo[:, at, :], aux_tiles(1)[:, 0:2, :], B_hi[:, at, :].bitcast(F32),
                                        ALU.subtract).then_inc(aux_drained[1], 1)

            def att_hooks(j):
                return ({0: lambda: q_start(j), 2: lambda: q_rows(j), 5: lambda: maxima(j, 0),
                         6: lambda: probs(j, 0)},
                        {0: lambda: maxima(j, 1), 1: lambda: o_lo(j, 0), 2: lambda: probs(j, 1),
                         7: lambda: o_lo(j, 1)})

            with links.loop(0, N4 - 1, 11) as j:
                first, second = att_hooks(j)
                chunk(Q_ATT + j * 2, first, j + 5, (0, 16))
                chunk(Q_ATT + 1 + j * 2, second, j + 5, (16, 32))
            first, second = att_hooks(N4 - 1)
            chunk(Q_AP - 2, first, N4 + 4, (0, 16))
            chunk(Q_AP - 1, second, N4 + 4, (16, 32))

            def gate_attention(c, j, group):
                cols = ds(group * COLS, COLS)
                dve.wait_ge(piece_used, (c + 1) * PIECES + j * 16)
                nc.vector.tensor_tensor(gates_a[:, :, cols], gates_a[:, :, cols], acc(c % 2),
                                        ALU.mult).then_inc(evacuated[c % 2], 1)

            with dve.Fori(0, N4 - 1) as j:
                chunk(Q_AP + j * 2, {}, j * 2 + N4 + 5, (0, 32))
                gate_attention(Q_AP, j, j)
                chunk(Q_AP + 1 + j * 2, {}, j * 2 + N4 + 6, (0, 32))
            chunk(Q_CP - 1, {}, KT - 1, (0, 32))
            gate_attention(Q_CP - 1, 0, N4 - 1)

            dve.wait_ge(aux_written[0], AUX0_LN + 1)
            mean = ps[:, 4, 0:SEQ]
            for c in range(4):
                y = glu[:, 4 * c:4 * c + 4, PAD:]
                last = nc.vector.tensor_tensor(y, y, mean.unsqueeze(1).to_broadcast([P, 4, SEQ]), ALU.subtract)
                last.then_inc(centred if c < 3 else aux_drained[0], 1)
            dve.wait_ge(aux_drained[0], AUX0_LN + 1)
            dve.wait_ge(aux_written[1], AUX1_LN + 1)
            nc.vector.tensor_scalar(conv_acc[:, 0, :], ps[:, 6, 0:SEQ], EPS, None, ALU.add).then_inc(aux_drained[1], 1)
            dve.wait_ge(var_sd, 1)
            link(nc.vector.reciprocal(conv_acc[:, 0, :], conv_acc[:, 1, :]))
            for c in range(4):
                y = glu[:, 4 * c:4 * c + 4, PAD:]
                nc.vector.tensor_tensor(y, y, conv_acc[:, 0:1, :].to_broadcast([P, 4, SEQ]),
                                        ALU.mult).then_inc(ln_scaled, 1)
            for c in range(4):
                dve.wait_ge(conv_hi, c + 1)
                nc.vector.tensor_tensor(A_lo[:, 4 * c:4 * c + 4, :], glu[:, 4 * c:4 * c + 4, PAD:],
                                        A_hi[:, 4 * c:4 * c + 4, :].bitcast(F32), ALU.subtract).then_inc(conv_lo, 1)

            def mix_rows(c):
                q = Q_CP + c
                cols = slice(c * COLS, (c + 1) * COLS)
                dve.wait_ge(piece_used, (q + 1) * PIECES)
                left_psum(dve, Q_CP - 2)
                nc.vector.tensor_tensor(mix_n, gates_b[:, :, cols], acc(q % 2), ALU.mult).then_inc(evacuated[q % 2], 1)
                dve.wait_ge(evacuated[q % 2], q // 2 + 1)
                nc.vector.tensor_tensor(mix_n, mix_n, gates_a[:, :, cols], ALU.add).then_inc(mix_ready, 1)

            def mix_lo(c):
                dve.wait_ge(mix_hi, c + 1)
                nc.vector.tensor_tensor(B_lo[:, 4 * c:4 * c + 4, :], aux_tiles(c % 2),
                                        B_hi[:, 4 * c:4 * c + 4, :].bitcast(F32),
                                        ALU.subtract).then_inc(aux_drained[c % 2], 1)

            for c in range(N4):
                chunk(Q_CP + c, {4: lambda: mix_lo(c - 1)} if c else {})
                mix_rows(c)

            def residual(c):
                q = Q_OUT + c
                cols = slice(c * COLS, (c + 1) * COLS)
                dve.wait_ge(piece_used, (q + 1) * PIECES)
                nc.vector.tensor_tensor(xres[:, :, cols], xres[:, :, cols], acc(q % 2),
                                        ALU.add).then_inc(evacuated[q % 2], 1)

            chunk(Q_OUT, {3: lambda: mix_lo(N4 - 1)})
            dve.wait_ge(x_reloaded, 16)
            residual(0)
            for c in range(1, N4):
                chunk(Q_OUT + c)
                residual(c)
            norm(1, (AUX0_NORM2, AUX1_NORM2), A_hi, A_lo, V_FFN)

            def ffn_taps(b, uses, dst, col, k):
                if k == 2:
                    dve.wait_ge(aux_written[b], uses)
                d = 2 - k
                for m in range(4):
                    w = ffn_dw[:, k, ds(col + m, 1)]
                    src = aux_tiles(b)[:, m, 0:SEQ - d]
                    if d == 0:
                        last = nc.vector.tensor_scalar(dst[:, m, :], src, w, None, ALU.mult)
                    else:
                        last = nc.vector.scalar_tensor_tensor(out=dst[:, m, d:], in0=src, scalar=w,
                                                              in1=dst[:, m, d:], op0=ALU.mult, op1=ALU.add)
                if k > 0:
                    link(last)
                return last

            def conv_g(j, k):
                last = ffn_taps(0, AUX0_UP + 1 + j, g_t, j * 4, k)
                if k == 0:
                    last.then_inc(aux_drained[0], 1)

            def conv_val(j, k):
                last = ffn_taps(1, AUX1_UP + 1 + j, val_t, j * 4 + FT, k)
                if k == 0:
                    last.then_inc(aux_drained[1], 1)
                    dve.wait_ge(aux_drained[1], AUX1_UP + 1 + j)

            def gated(j):
                dve.wait_ge(g_silu, j + 1)
                nc.vector.tensor_tensor(ff[:, ds(j * 4, 4), :], g_t, val_t, ALU.mult).then_inc(ff_ready, 1)

            def g_hooks(j):
                return {2: lambda: conv_g(j, 2), 3: lambda: conv_g(j, 1), 4: lambda: conv_g(j, 0)}

            def val_hooks(j):
                return {2: lambda: conv_val(j, 2), 3: lambda: conv_val(j, 1), 4: lambda: conv_val(j, 0),
                        5: lambda: gated(j)}

            chunk(Q_UP)
            with links.loop(0, UP_PAIRS - 1, 4) as j:
                chunk(Q_UP + 1 + j * 2, g_hooks(j))
                chunk(Q_UP + 2 + j * 2, val_hooks(j))
            chunk(Q_DOWN - 1, g_hooks(UP_PAIRS - 1))

            def ff_lo(kt, s, n):
                dve.wait_ge(ff_hi_ready, n)
                nc.vector.tensor_tensor(B_lo[:, s:s + 1, :], ff[:, ds(kt, 1), :], B_hi[:, s:s + 1, :].bitcast(F32),
                                        ALU.subtract).then_inc(ff_lo_ready, 1)

            for n in range(2):
                ff_lo(n, n, n + 1)
            for k in (2, 1, 0):
                conv_val(UP_PAIRS - 1, k)
            gated(UP_PAIRS - 1)
            with dve.Fori(0, N_DOWN - 1) as it:
                for i in range(PIECES):
                    split_lo(Q_DOWN + it, i)
                    if i % 2 == 0:
                        ff_lo(it * 4 + 2 + i // 2, (2 + i // 2) % 4, it * 4 + 3 + i // 2)
            for i in range(PIECE_LEAD):
                split_lo(Q_END - 1, i)
                if i % 2 == 0:
                    ff_lo(FT - 2 + i // 2, 2 + i // 2, FT - 1 + i // 2)
            for n in range(N4):
                for t in range(TT):
                    if n % 2 and t == TT - 1:
                        dve.wait_ge(piece_used, Q_END * PIECES - 1 + n // 2)
                    else:
                        dve.wait_ge(bank_done, n // 2 * 3 + n % 2 * TT + t + 1)
                    cols = slice(n * COLS, (n + 1) * COLS)
                    nc.vector.tensor_tensor(xres[:, t, cols], xres[:, t, cols], ps[:, t * N4 + n, :],
                                            ALU.add).then_inc(y_ready, 1)

        @block.tensor
        def _(pe):
            def piece(q, i, par, stat, first, last):
                s = i % PIECE_LEAD
                pe.wait_ge(lo_ready, q * PIECES + i + 1)
                for r in range(2):
                    k = 2 * i + r
                    hi, lo = w_hi[:, s, r * COLS:(r + 1) * COLS], w_lo[:, s, r * COLS:(r + 1) * COLS]
                    for t in range(TT):
                        o = ps[:, 2 * par + t, :]
                        a_hi, a_lo = (a[:, k, t * P:(t + 1) * P] for a in stat)
                        pe.matmul(o, a_hi, hi, start=(first and r == 0), stop=False)
                        pe.matmul(o, a_hi, lo, start=False, stop=False)
                        ins = pe.matmul(o, a_lo, hi, start=False, stop=(last and r == 1))
                ins.then_inc(piece_used, 1)

            def chunk(c, j, stat, hooks={}):
                if not (isinstance(j, int) and c + 2 * j < 2):
                    pe.wait_ge(evacuated[c % 2], j + c // 2)
                for i in range(PIECES):
                    if i in hooks:
                        hooks[i]()
                    piece(c + j * 2, i, c % 2, stat, i == 0, i == PIECES - 1)

            def aux_free(b, uses):
                pe.wait_ge(aux_drained[b], uses)

            def transpose_rows(b, uses, src, m=4):
                aux_free(b, uses)
                for n in range(m):
                    for t in range(TT):
                        last = pe.transpose(aux_tiles(b)[:, n, t * P:(t + 1) * P], src[:, t, n * P:(n + 1) * P], ident[:])
                last.then_inc(aux_written[b], 1)

            pe.wait_ge(consts_ready, 1)
            pe.wait_ge(params_landed, 12 * 16)
            for m in range(KT):
                pe.transpose(ps[:, 4, m * 32:m * 32 + TAPS], rows_dw[:, m * P:(m + 1) * P], ident[0:TAPS, 0:TAPS])
            pe.transpose(ps[:, 5, 0:NVEC], rows_vec, ident[0:NVEC, 0:NVEC])
            for k in range(3):
                last = pe.transpose(ps[:, 5, P + k * 2 * FT:P + (k + 1) * 2 * FT], rows_ffn[:, k, :],
                                    ident[0:2 * FT, 0:2 * FT])
            last.then_inc(aux_written[0], 1)

            def norm(first_stat, aux_base):
                for c in range(4):
                    pe.wait_ge(xn_ready, 8 * first_stat + 2 * c + 2)
                    n = aux_base[c % 2] + c // 2
                    if n:
                        transpose_rows(c % 2, n, xn[c % 2])
                    else:
                        for m in range(4):
                            for t in range(TT):
                                last = pe.transpose(aux_tiles(1)[:, m, t * P:(t + 1) * P],
                                                    xn[1][:, t, m * P:(m + 1) * P], ident[:])
                        last.then_inc(aux_written[1], 1)

            def normed(aux_base, c):
                pe.wait_ge(aux_drained[c % 2], aux_base[c % 2] + c // 2 + 1)

            A, B = (A_hi, A_lo), (B_hi, B_lo)
            norm(0, (AUX0_NORM1, AUX1_NORM1))

            def glu_in(j):
                pe.wait_ge(glu_ready, j + 1)
                transpose_rows(0, j + AUX0_GLU, stage2)

            base = (AUX0_NORM1, AUX1_NORM1)
            chunk(Q_U, 0, A, {2 * c: (lambda c=c: normed(base, c)) for c in range(4)})
            chunk(Q_U + 1, 0, A)
            chunk(Q_U + 2, 0, A, {2: lambda: glu_in(0)})
            with pe.Fori(1, N4 - 1) as j:
                chunk(Q_U + 1, j, A)
                chunk(Q_U + 2, j, A, {2: lambda: glu_in(j)})
            chunk(Q_KV - 1, 0, A)
            chunk(Q_KV, 0, A, {2: lambda: glu_in(N4 - 1)})

            def k_in():
                pe.wait_ge(k_ready, 1)
                aux_free(1, AUX1_KV)
                for g in range(KV_HEADS):
                    for t in range(TT):
                        last = pe.transpose(aux_tiles(1)[:, g, t * P:(t + 1) * P], stage2[:, t, g * P:(g + 1) * P],
                                            ident[:])
                last.then_inc(aux_written[1], 1)

            chunk(Q_Q0, 0, A, {3: k_in})

            def q_in(j):
                pe.wait_ge(qn_ready, j + 1)
                transpose_rows(1, j * 4 + AUX1_ATT, stage2)

            def scores(j, e):
                if e == 0:
                    pe.wait_ge(aux_drained[1], j * 4 + AUX1_ATT + 1)
                aux_free(e, (j * 3 + AUX0_ATT, j * 4 + AUX1_ATT + 1)[e])
                pe.transpose(ps[:, 4 + 2 * e, 0:P], ident[:], ident[:])
                for n in range(4):
                    pair, half = 2 * e + n // 2, 64 * (n % 2)
                    for c in range(NCHUNK):
                        rows = slice(64 * (c % 2), 64 * (c % 2) + 64)
                        cols = (n // 2) * 256 + (c // 2) * P
                        last = pe.matmul(ps[rows, 4 + 2 * e + n % 2, cols:cols + P],
                                         q_t[half:half + 64, pair, c * CHUNK:(c + 1) * CHUNK],
                                         k_head[half:half + 64, c * CHUNK:c * CHUNK + P], start=True, stop=True)
                last.then_inc(aux_written[e], 1)

            def probs_in(j, e):
                pe.wait_ge(prob_ready, j * 2 + e + 1)
                aux_free(0, j * 3 + AUX0_ATT + 1 + e)
                p = (prob0, prob1)[e]
                for n in range(8):
                    last = pe.transpose(aux(0).rearrange("p b n -> p (b n)")[:, n * P:(n + 1) * P],
                                        p[:, n * P:(n + 1) * P], ident[:])
                last.then_inc(aux_written[0], 1)

            def values(j, e):
                pe.wait_ge(aux_drained[0], j * 3 + AUX0_ATT + 2 + e)
                aux_free(1, j * 4 + AUX1_ATT + 2 + e)
                for n in range(4):
                    half, at = 64 * (n % 2), score_place(n) * 256
                    for c in range(NCHUNK):
                        cols = (n // 2) * SEQ + c * CHUNK
                        last = pe.matmul(ps[half:half + 64, 6, cols:cols + CHUNK], v_head[:, c, :],
                                         prob_t[:, at + c * CHUNK:at + (c + 1) * CHUNK],
                                         start=True, stop=True)
                last.then_inc(aux_written[1], 1)

            def att_hooks(j):
                return ({3: lambda: q_in(j), 4: lambda: (scores(j, 0), scores(j, 1)), 7: lambda: probs_in(j, 0)},
                        {0: lambda: values(j, 0), 4: lambda: probs_in(j, 1), 5: lambda: values(j, 1)})

            with pe.Fori(0, N4 - 1) as j:
                first, second = att_hooks(j)
                chunk(Q_ATT, j, A, first)
                chunk(Q_ATT + 1, j, A, second)
            first, second = att_hooks(N4 - 1)
            chunk(Q_AP - 2, 0, A, first)
            chunk(Q_AP - 1, 0, A, second)

            pe.wait_ge(aux_drained[1], AUX1_LN)
            with pe.Fori(0, N4 - 1) as j:
                chunk(Q_AP, j, B)
                chunk(Q_AP + 1, j, A)
            chunk(Q_CP - 1, 0, B)

            def channel_mean(dst, src, m):
                return pe.matmul(dst, mean_of[:], src, start=(m == 0), stop=(m == KT - 1))

            pe.wait_ge(consts_done, 1)
            pe.wait_ge(conv_tap, 32 * KT)
            aux_free(0, AUX0_LN)
            for m in range(KT):
                last = channel_mean(ps[:, 4, 0:SEQ], glu[:, m, PAD:], m)
            last.then_inc(aux_written[0], 1)
            for m in range(KT):
                if m % 4 == 0:
                    pe.wait_ge(squared, m // 4 + 1)
                last = channel_mean(ps[:, 6, 0:SEQ], squares[:, m, :], m)
            last.then_inc(aux_written[1], 1)

            def mix_in(c):
                pe.wait_ge(mix_ready, c + 1)
                transpose_rows(c % 2, (AUX0_MIX, AUX1_MIX)[c % 2] + c // 2, mix_n)

            for c in range(N4):
                hooks = {2: lambda: mix_in(c - 1)} if c else {2 * g: (lambda g=g: pe.wait_ge(conv_lo, g + 1))
                                                             for g in range(4)}
                chunk(Q_CP + c, 0, A, hooks)

            def mixed(c):
                pe.wait_ge(aux_drained[c % 2], (AUX0_MIX, AUX1_MIX)[c % 2] + c // 2 + 1)

            mixed(0), mixed(1), mixed(2)
            chunk(Q_OUT, 0, B, {1: lambda: mix_in(N4 - 1), 6: lambda: mixed(N4 - 1)})
            for c in range(1, N4):
                chunk(Q_OUT + c, 0, B)

            base2 = (AUX0_NORM2, AUX1_NORM2)
            norm(1, base2)

            def up_in(b, uses, c, j=0):
                left_psum(pe, c, j)
                transpose_rows(b, uses, up_n)

            chunk(Q_UP, 0, A, {2 * c: (lambda c=c: normed(base2, c)) for c in range(4)})
            with pe.Fori(0, UP_PAIRS - 1) as j:
                chunk(Q_UP + 1, j, A, {1: lambda: up_in(0, j + AUX0_UP, Q_UP, j)})
                chunk(Q_UP + 2, j, A, {1: lambda: up_in(1, j + AUX1_UP, Q_UP + 1, j)})
            chunk(Q_DOWN - 1, 0, A, {1: lambda: up_in(0, AUX0_UP + UP_PAIRS - 1, Q_DOWN - 2)})
            up_in(1, AUX1_UP + UP_PAIRS - 1, Q_DOWN - 1)

            left_psum(pe, Q_DOWN - 2)
            left_psum(pe, Q_DOWN - 1)
            for b in range(2):
                pe.wait_ge(aux_drained[b], (AUX0_UP, AUX1_UP)[b] + UP_PAIRS)

            def down(it, first=False, last=False):
                for i in range(PIECES):
                    s = i % PIECE_LEAD
                    pe.wait_ge(lo_ready, (Q_DOWN + it) * PIECES + i + 1)
                    if i % 2 == 0:
                        pe.wait_ge(ff_lo_ready, it * 4 + i // 2 + 1)
                    kt = i // 2
                    st, sp_ = first and kt == 0, last and kt == 3
                    for r in range(2):
                        n = 2 * (i % 2) + r
                        hi, lo = w_hi[:, s, r * COLS:(r + 1) * COLS], w_lo[:, s, r * COLS:(r + 1) * COLS]
                        for t in range(TT):
                            o = ps[:, t * N4 + n, :]
                            a_hi, a_lo = (a[:, kt, t * P:(t + 1) * P] for a in B)
                            pe.matmul(o, a_hi, hi, start=st, stop=False)
                            pe.matmul(o, a_hi, lo, start=False, stop=False)
                            ins = pe.matmul(o, a_lo, hi, start=False, stop=sp_)
                            if sp_ and not (r == 1 and t == TT - 1):
                                ins.then_inc(bank_done, 1)
                    ins.then_inc(piece_used, 1)

            down(0, first=True)
            with pe.Fori(1, N_DOWN - 1) as it:
                down(it)
            down(N_DOWN - 1, last=True)


_INS = ['x', 'norm_mix_g', 'w_in', 'q_norm_g', 'k_norm_g', 'sinks', 'w_attn_proj', 'conv_dw_w', 'conv_dw_b',
        'conv_ln_g', 'conv_ln_b', 'w_conv_proj', 'w_out', 'norm_ffn_g', 'w_up', 'ffn_dw_w', 'w_down']
_OUTS = [((1, 256, 2048), 'float32')]


def kernel(**inputs):
    import numpy as _np
    import concourse.bacc as _bacc
    from concourse import mybir as _mybir
    from concourse.bass_utils import run_bass_kernel_spmd as _run

    nc = _bacc.Bacc("TRN2", target_bir_lowering=False, num_devices=1)
    arrays, args = {}, []
    for name in _INS:
        a = _np.ascontiguousarray(inputs[name])
        arrays[f"in_{name}_dram"] = a
        args.append(nc.dram_tensor(f"in_{name}_dram", a.shape, _mybir.dt.from_np(a.dtype), kind="ExternalInput").ap())
    for i, (shape, dtype) in enumerate(_OUTS):
        dt = _mybir.dt.from_np(_np.dtype(dtype))
        args.append(nc.dram_tensor(f"out_{i}_dram", shape, dt, kind="ExternalOutput").ap())
    trunk(nc, *args)
    r = _run(nc, [arrays], core_ids=[0])
    got = tuple(r.results[0][f"out_{i}_dram"] for i in range(len(_OUTS)))
    return got[0]
```

```python
from contextlib import ExitStack, contextmanager

import concourse.bass as bass
from concourse import mybir

ACT = mybir.ActivationFunctionType
ALU = mybir.AluOpType
AX_X = mybir.AxisListType.X
F32 = mybir.dt.float32
F32R = mybir.dt.float32r
ds = bass.ds

P = 128
D = 2048
SEQ = 256
TT = SEQ // P
KT = D // P
COLS = 512
HEADS, KV_HEADS, HD = 32, 4, 64
GROUP = HEADS // KV_HEADS
CHUNK = 64
NCHUNK = SEQ // CHUNK
TAPS = 31
PAD = TAPS - 1
FF = 5632
FT = FF // P
UP_PAIRS = FF // COLS
EPS = 1e-6
KV_W = KV_HEADS * HD

PIECES = 8
PIECE_LEAD = 4
N4 = D // COLS

COL_Q, COL_KV = 0, D
COL_A = D + 2 * KV_W
COL_GLU = COL_A + D
COL_GATE_A = COL_GLU + D
COL_GATE_B = COL_GATE_A + D

Q_U = 0
Q_KV = Q_U + 2 * N4
Q_Q0 = Q_KV + 1
Q_ATT = Q_Q0 + 1
Q_AP = Q_ATT + 2 * N4
Q_CP = Q_AP + 2 * N4 - 1
Q_OUT = Q_CP + N4
Q_UP = Q_OUT + N4
Q_DOWN = Q_UP + 2 * UP_PAIRS
N_DOWN = FT // 4
Q_END = Q_DOWN + N_DOWN

AUX_NORM1 = 0
AUX0_PARAMS = 2
AUX0_GLU = 3
AUX1_KV = 2
AUX0_ATT, AUX1_ATT = AUX0_GLU + N4, AUX1_KV + 1
AUX0_LN, AUX1_LN = AUX0_ATT + 3 * N4, AUX1_ATT + 4 * N4
AUX_MIX = AUX0_LN + 1
AUX_NORM2 = AUX_MIX + 2
AUX_UP = AUX_NORM2 + 2
assert AUX0_LN == AUX1_LN

DOWN_BANKS = ((2, 3), (4, 5), (0, 1), (6, 7))

V_DWB, V_LNG, V_LNB = 0, KT, 2 * KT
V_QG = 3 * KT
V_KG = V_QG + 1
NVEC = V_KG + 1


def score_place(n):
    return 2 * (n % 2) + n // 2


class Chain:

    def __init__(self, eng, sem):
        self.eng, self.sem, self.at, self.shift = eng, sem, 0, 0

    def link(self, ins):
        ins.then_inc(self.sem, 1)
        self.at += 1
        self.eng.wait_ge(self.sem, self.at + self.shift)

    @contextmanager
    def loop(self, first, end, per_trip):
        start = self.at
        with self.eng.Fori(first, end) as j:
            self.shift = (j - first) * per_trip
            yield j
        assert self.at - start == per_trip, (self.at - start, per_trip)
        self.at = start + per_trip * (end - first)
        self.shift = 0


def trunk(nc, x, norm_mix_g, w_in, q_norm_g, k_norm_g, sinks, w_attn_proj, conv_dw_w, conv_dw_b,
          conv_ln_g, conv_ln_b, w_conv_proj, w_out, norm_ffn_g, w_up, ffn_dw_w, w_down, out):
    ctx = ExitStack()
    with ctx:
        def sb(name, shape, dt=F32):
            return ctx.enter_context(nc.sbuf_tensor(name, shape, dt))

        def sem(name):
            return ctx.enter_context(nc.semaphore(name))

        raw = sb("raw", [P, PIECE_LEAD, 1024])
        w_hi = sb("w_hi", [P, PIECE_LEAD, 1024], F32R)
        w_lo = sb("w_lo", [P, PIECE_LEAD, 1024], F32R)
        A_hi, A_lo = sb("A_hi", [P, KT, SEQ], F32R), sb("A_lo", [P, KT, SEQ], F32R)
        B_hi, B_lo = sb("B_hi", [P, KT, SEQ], F32R), sb("B_lo", [P, KT, SEQ], F32R)
        xres = sb("xres", [P, TT, D])
        big = sb("big", [P, 2 * TT * D + KT * (PAD + SEQ)])
        gates_a = big[:, 0:TT * D].rearrange("p (t n) -> p t n", t=TT)
        gates_b = big[:, TT * D:2 * TT * D].rearrange("p (t n) -> p t n", t=TT)
        glu = big[:, 2 * TT * D:].rearrange("p (m t) -> p m t", m=KT)
        ff = big[:, 0:FT * SEQ].rearrange("p (m t) -> p m t", m=FT)
        flat = xres[:, :, :].rearrange("p t n -> p (t n)")
        stage1 = flat[:, 0:1024].rearrange("p (t n) -> p t n", t=TT)
        stage2 = flat[:, 1024:2048].rearrange("p (t n) -> p t n", t=TT)
        stage3 = flat[:, 2048:3072].rearrange("p (t n) -> p t n", t=TT)
        q_t = flat[:, 2048:3072].rearrange("p (m t) -> p m t", m=4)
        prob0 = flat[:, 3072:4096]
        squares = flat.rearrange("p (m t) -> p m t", m=KT)
        work1 = sb("work1", [P, 1024])
        work2 = sb("work2", [P, 1024])
        work3 = sb("work3", [P, 1024])
        prob1 = work1[:, :]
        prob_t = work2[:, :]
        v_band = work3[:, :].rearrange("p (c n) -> p c n", c=NCHUNK)
        scaled = [work1[:, :].rearrange("p (t n) -> p t n", t=TT), work2[:, :].rearrange("p (t n) -> p t n", t=TT)]
        mix_n = scaled[0]
        up_n = scaled[0]
        g_t = work2[:, :].rearrange("p (m t) -> p m t", m=4)
        val_t = work3[:, :].rearrange("p (m t) -> p m t", m=4)
        k_t = sb("k_t", [P, KV_HEADS, CHUNK + SEQ])
        k_head = sb("k_head", [P, CHUNK + SEQ])
        v_head = sb("v_head", [P, NCHUNK, HD])
        dist = sb("dist", [P, TT, P])
        dist_raw = sb("dist_raw", [P, TT * P])
        conv_acc = sb("conv_acc", [P, 2, SEQ])
        dw_t = sb("dw_t", [P, KT, TAPS])
        vecs = sb("vecs", [P, NVEC])
        q_gain = sb("q_gain", [P, 1])
        ffn_dw = sb("ffn_dw", [P, 3, 2 * FT])
        neg_slope = sb("neg_slope", [P, HEADS])
        sink_rows = sb("sink_rows", [P, HEADS])
        sink = sb("sink", [P, HEADS])
        ident = sb("ident", [P, P])
        mean_of = sb("mean_of", [P, P])
        stats = sb("stats", [P, 96])
        rms_ms, rms_sd, rms_r, ssq_all = (stats[:, 2 * n:2 * n + 2] for n in range(4))
        ssq = stats[:, 8:16].rearrange("p (t c) -> p t c", t=TT)
        hs_sum, hs_ms, hs_sd, hs_r = (stats[:, 16 + 16 * n:32 + 16 * n] for n in range(4))
        soft = sb("soft", [P, 2, 6, 8])

        ps = ctx.enter_context(nc.psum_tensor("ps", [P, 8, COLS], F32))

        def acc(par):
            return ps[:, 2 * par:2 * par + 2, :]

        def aux(b):
            return ps[:, 4 + 2 * b:6 + 2 * b, :]

        def aux_tiles(b, m=4):
            return aux(b).rearrange("p b n -> p (b n)").rearrange("p (m t) -> p m t", m=m)

        rows_dw = big[0:TAPS, 0:D]
        rows_vec = big[0:NVEC, D:D + P]
        rows_ffn = big[0:2 * FT, D + P:D + 4 * P].rearrange("p (k n) -> p k n", k=3)
        junk = gates_b
        gain = big[:, 2 * TT * D:2 * TT * D + D]

        raw_landed = [sem(f"raw_landed{i}") for i in range(PIECE_LEAD)]
        hi_ready, lo_ready, piece_used = sem("hi_ready"), sem("lo_ready"), sem("piece_used")
        evacuated = [sem("evacuated_even"), sem("evacuated_odd")]
        aux_written = [sem("aux_written0"), sem("aux_written1")]
        aux_drained = [sem("aux_drained0"), sem("aux_drained1")]
        x_landed = [sem(f"x_landed{c}") for c in range(N4)]
        gain_landed, params_landed, x_reloaded = sem("gain_landed"), sem("params_landed"), sem("x_reloaded")
        consts_ready, iota_ready, consts_done = sem("consts_ready"), sem("iota_ready"), sem("consts_done")
        pool_step = sem("pool_step")
        dve_step = sem("dve_step")
        ssq_ready, ms_ready, sd_ready, rms_ready, scaled_ready, scaled_hi, h_ready = (sem(n) for n in (
            "ssq_ready", "ms_ready", "sd_ready", "rms_ready", "scaled_ready", "scaled_hi", "h_ready"))
        glu_ready = sem("glu_ready")
        k_ready, v_shifted = sem("k_ready"), sem("v_shifted")
        hs_squared, hs_ms_ready, hs_sd_ready, qn_ready = (sem(n) for n in (
            "hs_squared", "hs_ms_ready", "hs_sd_ready", "qn_ready"))
        max_ready, exp_ready, prob_ready, o_hi_ready = (sem(n) for n in (
            "max_ready", "exp_ready", "prob_ready", "o_hi_ready"))
        conv_tap = sem("conv_tap")
        centred, squared, var_sd, ln_scaled, ln_silu, conv_hi, conv_lo = (sem(n) for n in (
            "centred", "squared", "var_sd", "ln_scaled", "ln_silu", "conv_hi", "conv_lo"))
        mix_ready, mix_hi = sem("mix_ready"), sem("mix_hi")
        g_silu, ff_ready = sem("g_silu"), sem("ff_ready")
        ff_hi_ready, ff_lo_ready = sem("ff_hi_ready"), sem("ff_lo_ready")
        bank_done, y_ready, stored = sem("bank_done"), sem("y_ready"), sem("stored")

        block = ctx.enter_context(nc.Block())

        def left_psum(eng, c, j=0):
            eng.wait_ge(evacuated[c % 2], j + (c // 2 + 1))

        @block.sync
        def _(sp):
            x_rows = x[0].rearrange("(t p) n -> p t n", p=P)

            def load_x(c):
                cols = slice(c * COLS, (c + 1) * COLS)
                sp.dma_start(xres[:, :, cols], x_rows[:, :, cols]).then_inc(x_landed[c], 16)

            load_x(0)
            load_x(1)

            def load_chunk(q, w, c0, first=0):
                rows = w.rearrange("(i r p) n -> i p r n", r=2, p=P)
                for i in range(PIECES):
                    if first and i in (1, 2):
                        load_x(i + 1)
                    if i >= first:
                        sp.wait_ge(lo_ready, q * PIECES + i - (PIECE_LEAD - 1))
                    sp.dma_start(raw[:, i % PIECE_LEAD, :].rearrange("p (r n) -> p r n", r=2),
                                 rows[i][:, :, ds(c0, COLS)]).then_inc(raw_landed[i % PIECE_LEAD], 16)

            wi = w_in[0]
            load_chunk(Q_U, wi, COL_A, first=PIECE_LEAD)
            with sp.Fori(0, N4 - 1) as j:
                load_chunk(Q_U + 1 + j * 2, wi, COL_GLU + j * COLS)
                load_chunk(Q_U + 2 + j * 2, wi, COL_A + COLS + j * COLS)
            load_chunk(Q_KV - 1, wi, COL_GLU + (N4 - 1) * COLS)
            load_chunk(Q_KV, wi, COL_KV)
            load_chunk(Q_Q0, wi, COL_Q)
            with sp.Fori(0, N4 - 1) as j:
                load_chunk(Q_ATT + j * 2, wi, COL_GATE_A + j * COLS)
                load_chunk(Q_ATT + 1 + j * 2, wi, COL_Q + COLS + j * COLS)
            load_chunk(Q_AP - 2, wi, COL_GATE_A + (N4 - 1) * COLS)
            load_chunk(Q_AP - 1, wi, COL_GATE_B)
            with sp.Fori(0, N4 - 1) as j:
                load_chunk(Q_AP + j * 2, w_attn_proj[0], j * COLS)
                load_chunk(Q_AP + 1 + j * 2, wi, COL_GATE_B + COLS + j * COLS)
            load_chunk(Q_CP - 1, w_attn_proj[0], (N4 - 1) * COLS)
            with sp.Fori(0, N4) as j:
                load_chunk(Q_CP + j, w_conv_proj[0], j * COLS)
            sp.wait_ge(conv_lo, 4)
            sp.dma_start(xres[:], x_rows).then_inc(x_reloaded, 16)
            sp.dma_start(gain, norm_ffn_g.partition_broadcast(P)).then_inc(gain_landed, 16)
            with sp.Fori(0, N4) as j:
                load_chunk(Q_OUT + j, w_out[0], j * COLS)
            with sp.Fori(0, UP_PAIRS) as j:
                load_chunk(Q_UP + j * 2, w_up[0], j * COLS)
                load_chunk(Q_UP + 1 + j * 2, w_up[0], FF + j * COLS)
            down_rows = w_down[0].rearrange("(k p) n -> p k n", p=P)
            with sp.Fori(0, N_DOWN) as it:
                for i in range(PIECES):
                    sp.wait_ge(lo_ready, (Q_DOWN + it) * PIECES + i - (PIECE_LEAD - 1))
                    half = i // 4
                    sp.dma_start(raw[:, i % PIECE_LEAD:i % PIECE_LEAD + 1, :],
                                 down_rows[:, ds(it * 4 + i % 4, 1), half * 1024:(half + 1) * 1024]
                                 ).then_inc(raw_landed[i % PIECE_LEAD], 16)
            dst = out[0].rearrange("(t p) n -> p t n", p=P)
            for n in range(N4):
                for t in range(TT):
                    sp.wait_ge(y_ready, n * TT + t + 1)
                    sp.dma_start(dst[:, t, n * COLS:(n + 1) * COLS],
                                 xres[:, t, n * COLS:(n + 1) * COLS]).then_inc(stored, 16)
            sp.wait_ge(stored, 16 * N4 * TT)

        @block.gpsimd
        def _(pool):
            n = 0

            def step(ins):
                nonlocal n
                ins.then_inc(pool_step, 1)
                n += 1
                pool.wait_ge(pool_step, n)

            step(nc.gpsimd.memset(ident[:], 0.0))
            nc.gpsimd.affine_select(out=ident[:], in_=ident[:], compare_op=ALU.not_equal, fill=1.0, base=0,
                                    pattern=[[-1, P]], channel_multiplier=1).then_inc(consts_ready, 1)
            pool.wait_ge(consts_ready, 1)
            for half in range(2):
                nc.gpsimd.iota(dist_raw[64 * half:64 * half + 64, :].rearrange("p (t s) -> p t s", t=TT),
                               pattern=[[0, TT], [-1, P]], base=CHUNK, channel_multiplier=1,
                               allow_small_or_imprecise_dtypes=True).then_inc(iota_ready, 1)
                pool.wait_ge(iota_ready, half + 1)
            step(nc.gpsimd.memset(mean_of[:], 1.0 / D))
            for h in range(HEADS):
                at = h // 4 * 4 + score_place(h % 4)
                step(nc.gpsimd.memset(neg_slope[:, at:at + 1], -(2.0 ** (-8.0 * (h + 1) / HEADS))))
            nc.gpsimd.memset(k_t[:, :, 0:CHUNK], 0.0).then_inc(consts_done, 1)

        @block.scalar
        def _(act):
            def split_hi(q, i):
                s = i % PIECE_LEAD
                act.wait_ge(raw_landed[s], (q * 2 + 2 + i // PIECE_LEAD) * 16)
                act.wait_ge(piece_used, q * PIECES + i + 1)
                nc.scalar.activation(w_hi[:, s, :], raw[:, s, :], ACT.Copy).then_inc(hi_ready, 1)

            def chunk(q, hooks={}):
                for i in range(PIECES):
                    if i in hooks:
                        hooks[i]()
                    split_hi(q, i)

            def finished(q):
                act.wait_ge(piece_used, (q + 1) * PIECES)

            def rows_hi(base, c):
                act.wait_ge(aux_written[c % 2], base + c // 2 + 1)
                nc.scalar.activation(A_hi[:, 4 * c:4 * c + 4, :], aux_tiles(c % 2), ACT.Copy).then_inc(scaled_hi, 1)

            def root(n):
                act.wait_ge(ms_ready, n + 1)
                nc.scalar.activation(rms_sd, rms_ms, ACT.Sqrt).then_inc(sd_ready, 1)

            act.dma_start(gain, norm_mix_g.partition_broadcast(P)).then_inc(gain_landed, 16)
            for n, v in enumerate((conv_dw_b, conv_ln_g, conv_ln_b)):
                act.dma_start(rows_vec[n * KT:(n + 1) * KT, :],
                              v[0].rearrange("(m n) -> m n", n=P)).then_inc(params_landed, 16)
            for n, v in enumerate((q_norm_g, k_norm_g)):
                for half in range(2):
                    act.dma_start(rows_vec[V_QG + n:V_QG + n + 1, half * HD:(half + 1) * HD],
                                  v).then_inc(params_landed, 16)
            act.dma_start(rows_dw, conv_dw_w[0]).then_inc(params_landed, 16)
            act.dma_start(rows_ffn, ffn_dw_w[0].rearrange("k (m n) -> m k n", n=P)).then_inc(params_landed, 16)
            act.dma_start(sink_rows[:], sinks.partition_broadcast(P)).then_inc(params_landed, 16)

            for i in range(PIECE_LEAD):
                act.wait_ge(raw_landed[i], 16)
                nc.scalar.activation(w_hi[:, i, :], raw[:, i, :], ACT.Copy).then_inc(hi_ready, 1)
                if i < 2:
                    rows_hi(AUX_NORM1, i)

            def square_x():
                for t in range(TT):
                    for c in range(N4):
                        act.wait_ge(x_landed[c], 16)
                    nc.scalar.activation(junk[:, t, :], xres[:, t, :], ACT.Square,
                                         accum_out=ssq_all[:, t:t + 1]).then_inc(ssq_ready, 1)

            def glu_out(j):
                act.wait_ge(aux_written[0], AUX0_GLU + 1 + j)
                nc.scalar.activation(glu[:, ds(j * 4, 4), PAD:], aux_tiles(0), ACT.Copy).then_inc(aux_drained[0], 1)

            def evac(c, j, dst, func):
                finished(c + j * 2)
                for t in range(TT):
                    last = nc.scalar.activation(dst[:, t, :], acc(c % 2)[:, t, :], func, scale=rms_r[:, t:t + 1])
                last.then_inc(evacuated[c % 2], 1)

            def square_heads(c, j, width):
                left_psum(act, c, j)
                nc.scalar.activation(stage3[:, :, 0:width], stage1[:, :, 0:width], ACT.Square).then_inc(hs_squared, 1)

            chunk(Q_U, {1: lambda: rows_hi(AUX_NORM1, 2), 3: lambda: rows_hi(AUX_NORM1, 3), 4: square_x,
                        6: lambda: root(0)})
            act.wait_ge(rms_ready, 1)
            evac(Q_U, 0, stage1, ACT.Copy)
            with act.Fori(0, N4 - 1) as j:
                chunk(Q_U + 1 + j * 2)
                evac(Q_U + 1, j, stage3, ACT.Sigmoid)
                chunk(Q_U + 2 + j * 2, {3: lambda: glu_out(j)})
                evac(Q_U + 2, j, stage1, ACT.Copy)
            chunk(Q_KV - 1)
            evac(Q_KV - 1, 0, stage3, ACT.Sigmoid)
            chunk(Q_KV, {3: lambda: glu_out(N4 - 1)})
            evac(Q_KV, 0, stage1, ACT.Copy)
            square_heads(Q_KV, 0, KV_W)

            act.dma_start(v_band[64:P, 0, :], stage1[0:64, 0, KV_W:]).then_inc(v_shifted, 16)
            act.dma_start(v_band[0:64, 2, :], stage1[64:P, 0, KV_W:]).then_inc(v_shifted, 16)
            act.dma_start(v_band[64:P, 2, :], stage1[0:64, 1, KV_W:]).then_inc(v_shifted, 16)

            def head_root(n):
                act.wait_ge(hs_ms_ready, n + 1)
                nc.scalar.activation(hs_sd, hs_ms, ACT.Sqrt).then_inc(hs_sd_ready, 1)

            def k_out():
                act.wait_ge(aux_written[1], AUX1_KV + 1)
                nc.scalar.activation(k_t[:, :, CHUNK:], aux_tiles(1), ACT.Copy,
                                     scale=vecs[:, V_KG:V_KG + 1]).then_inc(aux_drained[1], 1)
                act.wait_ge(v_shifted, 48)

            chunk(Q_Q0, {1: lambda: head_root(0), 5: k_out})
            evac(Q_Q0, 0, stage1, ACT.Copy)
            square_heads(Q_Q0, 0, COLS)

            def q_out(j):
                act.wait_ge(aux_written[1], AUX1_ATT + 1 + j * 4)
                nc.scalar.activation(q_t, aux_tiles(1), ACT.Copy, scale=q_gain[:]).then_inc(aux_drained[1], 1)

            def exps(j, e):
                act.wait_ge(max_ready, j * 2 + e + 1)
                p = (prob0, prob1)[e]
                s = soft[:, e]
                for n in range(8):
                    nc.scalar.activation(p[:, n * P:(n + 1) * P], p[:, n * P:(n + 1) * P], ACT.Exp,
                                         bias=s[:, 1, n:n + 1], accum_out=s[:, 3, n:n + 1])
                nc.scalar.activation(s[:, 4, :], s[:, 2, :], ACT.Exp).then_inc(exp_ready, 1)

            def prob_out(j, e):
                act.wait_ge(aux_written[0], AUX0_ATT + 2 + e + j * 3)
                nc.scalar.activation(prob_t, aux(0).rearrange("p b n -> p (b n)"), ACT.Copy).then_inc(aux_drained[0], 1)

            def o_out(j, e):
                act.wait_ge(aux_written[1], AUX1_ATT + 3 + e + j * 4)
                nc.scalar.activation(B_hi[:, ds(j * 4 + 2 * e, 2), :], aux_tiles(1)[:, 0:2, :],
                                     ACT.Copy).then_inc(o_hi_ready, 1)

            def att_hooks(j):
                return ({1: lambda: head_root(j + 1), 5: lambda: q_out(j), 7: lambda: exps(j, 0)},
                        {1: lambda: exps(j, 1), 3: lambda: prob_out(j, 0),
                         5: lambda: (o_out(j, 0), prob_out(j, 1)), 7: lambda: o_out(j, 1)})

            with act.Fori(0, N4 - 1) as j:
                first, second = att_hooks(j)
                chunk(Q_ATT + j * 2, first)
                evac(Q_ATT, j, gates_a[:, :, ds(j * COLS, COLS)], ACT.Sigmoid)
                chunk(Q_ATT + 1 + j * 2, second)
                evac(Q_ATT + 1, j, stage1, ACT.Copy)
                square_heads(Q_ATT + 1, j, COLS)
            first, second = att_hooks(N4 - 1)
            chunk(Q_AP - 2, first)
            evac(Q_AP - 2, 0, gates_a[:, :, (N4 - 1) * COLS:], ACT.Sigmoid)
            chunk(Q_AP - 1, second)
            evac(Q_AP - 1, 0, gates_b[:, :, 0:COLS], ACT.Sigmoid)

            with act.Fori(0, N4 - 1) as j:
                chunk(Q_AP + j * 2)
                chunk(Q_AP + 1 + j * 2)
                evac(Q_AP + 1, j, gates_b[:, :, ds(COLS + j * COLS, COLS)], ACT.Sigmoid)

            def ln_squares():
                for c in range(4):
                    if c < 3:
                        act.wait_ge(centred, c + 1)
                    else:
                        act.wait_ge(aux_drained[0], AUX0_LN + 1)
                    nc.scalar.activation(squares[:, 4 * c:4 * c + 4, :], glu[:, 4 * c:4 * c + 4, PAD:],
                                         ACT.Square).then_inc(squared, 1)

            def ln_root():
                act.wait_ge(aux_drained[1], AUX1_LN + 1)
                nc.scalar.activation(conv_acc[:, 1, :], conv_acc[:, 0, :], ACT.Sqrt).then_inc(var_sd, 1)

            def ln_swish(c):
                act.wait_ge(ln_scaled, c + 1)
                for m in range(4 * c, 4 * c + 4):
                    last = nc.scalar.activation(glu[:, m, PAD:], glu[:, m, PAD:], ACT.Silu,
                                                scale=vecs[:, V_LNG + m:V_LNG + m + 1],
                                                bias=vecs[:, V_LNB + m:V_LNB + m + 1])
                last.then_inc(ln_silu, 1)

            chunk(Q_CP - 1, {3: ln_squares, 6: ln_root})
            ln_swish(0)

            def mix_out(c):
                act.wait_ge(aux_written[c % 2], AUX_MIX + c // 2 + 1)
                nc.scalar.activation(B_hi[:, 4 * c:4 * c + 4, :], aux_tiles(c % 2), ACT.Copy).then_inc(mix_hi, 1)

            for c in range(N4):
                chunk(Q_CP + c, {3: lambda: mix_out(c - 1)} if c else
                      {0: lambda: ln_swish(1), 1: lambda: ln_swish(2), 2: lambda: ln_swish(3)})

            def square_h(c):
                for t in range(TT):
                    nc.scalar.activation(junk[:, t, c * COLS:(c + 1) * COLS], xres[:, t, c * COLS:(c + 1) * COLS],
                                         ACT.Square, accum_out=ssq[:, t, c:c + 1]).then_inc(ssq_ready, 1)

            def h_out(c):
                rows_hi(AUX_NORM2, c)
                square_h(c)

            chunk(Q_OUT, {2: lambda: mix_out(N4 - 1)})
            for c in range(1, N4):
                chunk(Q_OUT + c, {2: lambda: h_out(c - 1)})

            def silu_g(j):
                act.wait_ge(aux_drained[0], j + AUX_UP + 1)
                nc.scalar.activation(g_t, g_t, ACT.Silu).then_inc(g_silu, 1)

            chunk(Q_UP, {2: lambda: h_out(N4 - 1), 5: lambda: root(1)})
            act.wait_ge(rms_ready, 2)
            evac(Q_UP, 0, up_n, ACT.Copy)
            with act.Fori(0, UP_PAIRS - 1) as j:
                chunk(Q_UP + 1 + j * 2, {6: lambda: silu_g(j)})
                evac(Q_UP + 1, j, up_n, ACT.Copy)
                chunk(Q_UP + 2 + j * 2)
                evac(Q_UP + 2, j, up_n, ACT.Copy)

            def split_ff(kt, s):
                nc.scalar.activation(B_hi[:, s:s + 1, :], ff[:, ds(kt, 1), :], ACT.Copy).then_inc(ff_hi_ready, 1)

            chunk(Q_DOWN - 1, {6: lambda: silu_g(UP_PAIRS - 1)})
            evac(Q_DOWN - 1, 0, up_n, ACT.Copy)
            act.wait_ge(ff_ready, 1)
            for n in range(4):
                split_ff(n, n)

            def down(it, last=False):
                for i in range(PIECE_LEAD if last else PIECES):
                    split_hi(Q_DOWN + it, i)
                    if i >= 4:
                        split_ff(it * 4 + i, i - 4)

            down(0)
            act.wait_ge(ff_ready, UP_PAIRS)
            with act.Fori(1, N_DOWN - 1) as it:
                down(it)
            down(N_DOWN - 1, last=True)

        @block.vector
        def _(dve):
            links = Chain(dve, dve_step)
            link = links.link

            def split_lo(q, i):
                s = i % PIECE_LEAD
                dve.wait_ge(hi_ready, q * PIECES + PIECE_LEAD + i + 1)
                nc.vector.tensor_tensor(w_lo[:, s, :], raw[:, s, :], w_hi[:, s, :].bitcast(F32),
                                        ALU.subtract).then_inc(lo_ready, 1)

            def chunk(q, hooks={}, taps_of=None, first_tap=0, taps=(4,) * PIECES):
                for i in range(PIECES):
                    if i in hooks:
                        hooks[i]()
                    split_lo(q, i)
                    if taps_of is not None:
                        conv_taps(taps_of, first_tap, first_tap + taps[i])
                        first_tap += taps[i]

            def conv_taps(m, k0, k1):
                tile = glu[:, ds(m, 1), :].rearrange("p m t -> p (m t)")
                for k in range(k0, k1):
                    a = conv_acc[:, k % 2, :]
                    if k >= 1:
                        dve.wait_ge(conv_tap, m * 32 + (k if k in (1, 30, 31) else k - 1))
                    if k < 31:
                        src = tile[:, k:k + SEQ]
                        w = dw_t[:, ds(m, 1), k:k + 1].rearrange("p m k -> p (m k)")
                    if k == 0:
                        bias = vecs[:, ds(m + V_DWB, 1)]
                        ins = nc.vector.tensor_scalar(a, src, w, bias, ALU.mult, ALU.add)
                    elif k == 1:
                        ins = nc.vector.tensor_scalar(a, src, w, None, ALU.mult)
                    elif k < 30:
                        ins = nc.vector.scalar_tensor_tensor(out=a, in0=src, scalar=w, in1=a,
                                                             op0=ALU.mult, op1=ALU.add)
                    elif k == 30:
                        ins = nc.vector.scalar_tensor_tensor(out=tile[:, PAD:], in0=src, scalar=w, in1=a,
                                                             op0=ALU.mult, op1=ALU.add)
                    else:
                        ins = nc.vector.tensor_tensor(tile[:, PAD:], tile[:, PAD:], a, ALU.add)
                    ins.then_inc(conv_tap, 1)

            def scale_rows(c):
                cols = slice(c * COLS, (c + 1) * COLS)
                nc.vector.tensor_tensor(scaled[c % 2], xres[:, :, cols],
                                        gain[:, cols].unsqueeze(1).to_broadcast([P, TT, COLS]),
                                        ALU.mult).then_inc(scaled_ready, 1)

            def rows_lo(n, c):
                dve.wait_ge(scaled_hi, 4 * n + c + 1)
                nc.vector.tensor_tensor(A_lo[:, 4 * c:4 * c + 4, :], aux_tiles(c % 2),
                                        A_hi[:, 4 * c:4 * c + 4, :].bitcast(F32),
                                        ALU.subtract).then_inc(aux_drained[c % 2], 1)

            def mean_squares(n, total):
                nc.vector.tensor_scalar(rms_ms, total, 1.0 / D, EPS, ALU.mult, ALU.add).then_inc(ms_ready, 1)

            def inverse(n):
                dve.wait_ge(sd_ready, n + 1)
                nc.vector.reciprocal(rms_r, rms_sd).then_inc(rms_ready, 1)

            def first_lo(i):
                dve.wait_ge(hi_ready, i + 1)
                nc.vector.tensor_tensor(w_lo[:, i, :], raw[:, i, :], w_hi[:, i, :].bitcast(F32),
                                        ALU.subtract).then_inc(lo_ready, 1)

            def scale_x(c):
                dve.wait_ge(x_landed[c], 16)
                scale_rows(c)

            dve.wait_ge(gain_landed, 16)
            scale_x(0)
            scale_x(1)
            first_lo(0)
            rows_lo(0, 0)
            first_lo(1)
            scale_x(2)
            rows_lo(0, 1)
            scale_x(3)
            first_lo(2)
            first_lo(3)

            def constants():
                dve.wait_ge(scaled_ready, N4)
                nc.vector.memset(glu[:, :, 0:PAD], 0.0)
                nc.vector.memset(v_band[0:64, 0, :], 0.0)
                dve.wait_ge(iota_ready, 2)
                link(nc.vector.scalar_tensor_tensor(
                    out=dist[:, :, :].rearrange("p t s -> p (t s)"), in0=dist_raw[:],
                    scalar=-1.0, in1=dist_raw[:], op0=ALU.mult, op1=ALU.max))
                link(nc.vector.memset(dist[0:CHUNK, 0, 0:CHUNK], 1e30))
                dve.wait_ge(params_landed, 10 * 16)
                nc.vector.tensor_copy(sink[:].rearrange("p (g b a) -> p g b a", a=2, b=2),
                                      sink_rows[:].rearrange("p (g a b) -> p g b a", a=2, b=2))

            def parameters():
                dve.wait_ge(aux_written[0], AUX0_PARAMS + 1)
                nc.vector.tensor_copy(dw_t[:], ps[:, 4, :].rearrange("p (m k) -> p m k", k=32)[:, :, 0:TAPS])
                link(nc.vector.tensor_copy(vecs[:], ps[:, 5, 0:NVEC]))
                nc.vector.tensor_scalar(q_gain[:], vecs[:, V_QG:V_QG + 1], HD ** -0.5, None, ALU.mult)
                nc.vector.tensor_copy(ffn_dw[:], ps[:, 5, P:P + 6 * FT].rearrange("p (k m) -> p k m", k=3)
                                      ).then_inc(aux_drained[0], 1)

            def rms_1():
                dve.wait_ge(ssq_ready, TT)
                mean_squares(0, ssq_all)

            def glu_product(j):
                left_psum(dve, Q_U + 1, j)
                nc.vector.tensor_tensor(stage2, stage1, stage3, ALU.mult).then_inc(glu_ready, 1)

            def glu_landed(m):
                dve.wait_ge(aux_drained[0], AUX0_GLU + 1 + m // 4)

            chunk(Q_U, {1: lambda: rows_lo(0, 2), 3: lambda: rows_lo(0, 3), 4: constants, 6: rms_1, 7: lambda: inverse(0)})
            chunk(Q_U + 1, {1: parameters})
            chunk(Q_U + 2, {0: lambda: glu_product(0)})
            with dve.Fori(1, N4 - 1) as j:
                chunk(Q_U + 1 + j * 2, {0: lambda: dve.wait_ge(aux_drained[0], AUX0_GLU + 1)}, j * 2 - 2)
                chunk(Q_U + 2 + j * 2, {0: lambda: glu_product(j)}, j * 2 - 1)
            chunk(Q_KV - 1, {0: lambda: dve.wait_ge(aux_drained[0], AUX0_GLU + 2)}, 4)
            chunk(Q_KV, {0: lambda: glu_product(N4 - 1)}, 5)

            def head_rms(n_heads, n):
                w = n_heads * HD
                dve.wait_ge(hs_squared, n + 1)
                for t in range(TT):
                    last = nc.vector.tensor_reduce(
                        hs_sum[:, t * n_heads:(t + 1) * n_heads],
                        stage3[:, t, 0:w].rearrange("p (h d) -> p h d", d=HD), AX_X, ALU.add)
                link(last)
                nh = TT * n_heads
                if nh < 16:
                    link(nc.vector.memset(hs_sum[:, nh:16], 1.0))
                nc.vector.tensor_scalar(hs_ms, hs_sum, 1.0 / HD, EPS, ALU.mult, ALU.add).then_inc(hs_ms_ready, 1)

            def head_inverse(n):
                dve.wait_ge(hs_sd_ready, n + 1)
                link(nc.vector.reciprocal(hs_r, hs_sd))

            def heads_of(r, t, n_heads):
                return r[:, t * n_heads:(t + 1) * n_heads].unsqueeze(2).to_broadcast([P, n_heads, HD])

            def k_start():
                dve.wait_ge(consts_done, 1)
                left_psum(dve, Q_KV)
                dve.wait_ge(aux_drained[0], AUX0_GLU + N4)
                for t in range(TT):
                    nc.vector.tensor_copy(v_band[:, 2 * t + 1, :], stage1[:, t, KV_W:])
                head_rms(KV_HEADS, 0)

            def k_rows():
                head_inverse(0)
                for t in range(TT):
                    for dup in range(2):
                        dst = stage2[:, t, :].rearrange("p (g u d) -> p g u d", u=2, d=HD)[:, :, dup, :]
                        last = nc.vector.tensor_tensor(dst, stage1[:, t, 0:KV_W].rearrange("p (g d) -> p g d", d=HD),
                                                       heads_of(hs_r, t, KV_HEADS), ALU.mult)
                last.then_inc(k_ready, 1)

            chunk(Q_Q0, {0: k_start, 3: k_rows}, 6)

            def q_start(j):
                left_psum(dve, Q_Q0, j)
                head_rms(GROUP, j + 1)

            def q_rows(j):
                head_inverse(j + 1)
                nc.vector.tensor_copy(v_head[:], v_band[:, :, ds(j * HD, HD)])
                nc.vector.tensor_copy(k_head[:], k_t[:, ds(j, 1), :].rearrange("p g t -> p (g t)"))
                for t in range(TT):
                    last = nc.vector.tensor_tensor(
                        stage2[:, t, :].rearrange("p (h d) -> p h d", d=HD),
                        stage1[:, t, :].rearrange("p (h d) -> p h d", d=HD), heads_of(hs_r, t, GROUP), ALU.mult)
                last.then_inc(qn_ready, 1)

            def maxima(j, e):
                b = e
                dve.wait_ge(aux_written[b], (AUX0_ATT + 1 + j * 3, AUX1_ATT + 2 + j * 4)[e])
                p = (prob0, prob1)[e]
                s = soft[:, e]
                for n in range(4):
                    last = nc.vector.scalar_tensor_tensor(
                        out=p[:, n * 256:(n + 1) * 256], in0=dist[:, :, :].rearrange("p t s -> p (t s)"),
                        scalar=neg_slope[:, ds(j * GROUP + 4 * e + n, 1)],
                        in1=aux(b).rearrange("p b n -> p (b n)")[:, n * 256:(n + 1) * 256],
                        op0=ALU.mult, op1=ALU.add)
                last.then_inc(aux_drained[b], 1)
                dve.wait_ge(aux_drained[b], (AUX0_ATT + 1 + j * 3, AUX1_ATT + 2 + j * 4)[e])
                link(nc.vector.tensor_reduce(s[:, 0, :], p.rearrange("p (n s) -> p n s", s=P), AX_X, ALU.max))
                sk = sink[:, ds(j * GROUP + 4 * e, 4)].unsqueeze(2).to_broadcast([P, 4, TT])
                m = s[:, 0, :].rearrange("p (n t) -> p n t", t=TT)
                link(nc.vector.tensor_tensor(m, m, sk, ALU.max))
                nc.vector.tensor_scalar(s[:, 1, :], s[:, 0, :], -1.0, None, ALU.mult)
                nc.vector.tensor_tensor(s[:, 2, :].rearrange("p (n t) -> p n t", t=TT), sk, m,
                                        ALU.subtract).then_inc(max_ready, 1)

            def probs(j, e):
                dve.wait_ge(exp_ready, j * 2 + e + 1)
                p = (prob0, prob1)[e].rearrange("p (n s) -> p n s", s=P)
                s = soft[:, e]
                link(nc.vector.tensor_tensor(s[:, 5, :], s[:, 3, :], s[:, 4, :], ALU.add))
                link(nc.vector.reciprocal(s[:, 0, :], s[:, 5, :]))
                nc.vector.tensor_tensor(p, p, s[:, 0, :].unsqueeze(2).to_broadcast([P, 8, P]),
                                        ALU.mult).then_inc(prob_ready, 1)

            def o_lo(j, e):
                dve.wait_ge(o_hi_ready, j * 2 + e + 1)
                at = ds(j * 4 + 2 * e, 2)
                nc.vector.tensor_tensor(B_lo[:, at, :], aux_tiles(1)[:, 0:2, :], B_hi[:, at, :].bitcast(F32),
                                        ALU.subtract).then_inc(aux_drained[1], 1)

            def att_hooks(j):
                return ({0: lambda: q_start(j), 3: lambda: q_rows(j), 6: lambda: maxima(j, 0)},
                        {0: lambda: maxima(j, 1), 1: lambda: probs(j, 0), 3: lambda: probs(j, 1),
                         5: lambda: o_lo(j, 0), 7: lambda: o_lo(j, 1)})

            first_taps, second_taps = (3, 4, 3, 0, 4, 4, 0, 0), (0, 0, 4, 0, 4, 0, 4, 2)
            with links.loop(0, N4 - 1, 10) as j:
                first, second = att_hooks(j)
                chunk(Q_ATT + j * 2, first, j + 7, 0, first_taps)
                chunk(Q_ATT + 1 + j * 2, second, j + 7, sum(first_taps), second_taps)
            first, second = att_hooks(N4 - 1)
            chunk(Q_AP - 2, first)
            chunk(Q_AP - 1, second)

            def gate_attention(c, j, group):
                cols = ds(group * COLS, COLS)
                dve.wait_ge(piece_used, (c + 1) * PIECES + j * 16)
                nc.vector.tensor_tensor(gates_a[:, :, cols], gates_a[:, :, cols], acc(c % 2),
                                        ALU.mult).then_inc(evacuated[c % 2], 1)

            with dve.Fori(0, N4 - 1) as j:
                chunk(Q_AP + j * 2, {}, j * 2 + KT - 6)
                gate_attention(Q_AP, j, j)
                chunk(Q_AP + 1 + j * 2, {}, j * 2 + KT - 5)

            def ln_centre():
                dve.wait_ge(aux_written[0], AUX0_LN + 1)
                mean = ps[:, 4, 0:SEQ]
                for c in range(4):
                    y = glu[:, 4 * c:4 * c + 4, PAD:]
                    nc.vector.tensor_tensor(y, y, mean.unsqueeze(1).to_broadcast([P, 4, SEQ]), ALU.subtract
                                            ).then_inc(centred if c < 3 else aux_drained[0], 1)

            def ln_variance():
                dve.wait_ge(aux_written[1], AUX1_LN + 1)
                nc.vector.tensor_scalar(conv_acc[:, 0, :], ps[:, 6, 0:SEQ], EPS, None, ALU.add
                                        ).then_inc(aux_drained[1], 1)

            def ln_scale():
                dve.wait_ge(var_sd, 1)
                link(nc.vector.reciprocal(conv_acc[:, 0, :], conv_acc[:, 1, :]))
                for c in range(4):
                    y = glu[:, 4 * c:4 * c + 4, PAD:]
                    nc.vector.tensor_tensor(y, y, conv_acc[:, 0:1, :].to_broadcast([P, 4, SEQ]),
                                            ALU.mult).then_inc(ln_scaled, 1)

            def ln_split(c):
                dve.wait_ge(ln_silu, c + 1)
                y, hi = glu[:, 4 * c:4 * c + 4, PAD:], A_hi[:, 4 * c:4 * c + 4, :]
                nc.vector.tensor_copy(hi, y).then_inc(conv_hi, 1)
                dve.wait_ge(conv_hi, c + 1)
                nc.vector.tensor_tensor(A_lo[:, 4 * c:4 * c + 4, :], y, hi.bitcast(F32),
                                        ALU.subtract).then_inc(conv_lo, 1)

            chunk(Q_CP - 1, {2: ln_centre, 6: ln_variance, 7: ln_scale})
            ln_split(0)
            gate_attention(Q_CP - 1, 0, N4 - 1)

            def mix_rows(c):
                q = Q_CP + c
                cols = slice(c * COLS, (c + 1) * COLS)
                dve.wait_ge(piece_used, (q + 1) * PIECES)
                left_psum(dve, Q_CP - 2)
                nc.vector.tensor_tensor(mix_n, gates_b[:, :, cols], acc(q % 2), ALU.mult).then_inc(evacuated[q % 2], 1)
                dve.wait_ge(evacuated[q % 2], q // 2 + 1)
                nc.vector.tensor_tensor(mix_n, mix_n, gates_a[:, :, cols], ALU.add).then_inc(mix_ready, 1)

            def mix_lo(c):
                dve.wait_ge(mix_hi, c + 1)
                nc.vector.tensor_tensor(B_lo[:, 4 * c:4 * c + 4, :], aux_tiles(c % 2),
                                        B_hi[:, 4 * c:4 * c + 4, :].bitcast(F32),
                                        ALU.subtract).then_inc(aux_drained[c % 2], 1)

            for c in range(N4):
                chunk(Q_CP + c, {4: lambda: mix_lo(c - 1)} if c else
                      {1: lambda: ln_split(1), 2: lambda: ln_split(2), 3: lambda: ln_split(3)})
                mix_rows(c)

            def residual(c):
                q = Q_OUT + c
                cols = slice(c * COLS, (c + 1) * COLS)
                dve.wait_ge(piece_used, (q + 1) * PIECES)
                nc.vector.tensor_tensor(xres[:, :, cols], xres[:, :, cols], acc(q % 2),
                                        ALU.add).then_inc(evacuated[q % 2], 1)
                left_psum(dve, q)
                scale_rows(c)

            def rms_2():
                dve.wait_ge(ssq_ready, TT + TT * N4)
                link(nc.vector.tensor_reduce(ssq_all, ssq, AX_X, ALU.add))
                mean_squares(1, ssq_all)

            chunk(Q_OUT, {3: lambda: mix_lo(N4 - 1)})
            dve.wait_ge(x_reloaded, 16)
            dve.wait_ge(gain_landed, 32)
            residual(0)
            for c in range(1, N4):
                chunk(Q_OUT + c, {3: lambda: rows_lo(1, c - 1)})
                residual(c)

            def ffn_taps(b, uses, dst, col, k):
                if k == 2:
                    dve.wait_ge(aux_written[b], uses)
                d = 2 - k
                for m in range(4):
                    w = ffn_dw[:, k, ds(col + m, 1)]
                    src = aux_tiles(b)[:, m, 0:SEQ - d]
                    if d == 0:
                        last = nc.vector.tensor_scalar(dst[:, m, :], src, w, None, ALU.mult)
                    else:
                        last = nc.vector.scalar_tensor_tensor(out=dst[:, m, d:], in0=src, scalar=w,
                                                              in1=dst[:, m, d:], op0=ALU.mult, op1=ALU.add)
                if k > 0:
                    link(last)
                return last

            def conv_g(j, k):
                last = ffn_taps(0, AUX_UP + 1 + j, g_t, j * 4, k)
                if k == 0:
                    last.then_inc(aux_drained[0], 1)

            def conv_val(j, k):
                last = ffn_taps(1, AUX_UP + 1 + j, val_t, j * 4 + FT, k)
                if k == 0:
                    last.then_inc(aux_drained[1], 1)
                    dve.wait_ge(aux_drained[1], AUX_UP + 1 + j)

            def gated(j):
                dve.wait_ge(g_silu, j + 1)
                nc.vector.tensor_tensor(ff[:, ds(j * 4, 4), :], g_t, val_t, ALU.mult).then_inc(ff_ready, 1)

            def g_hooks(j):
                return {2: lambda: conv_g(j, 2), 3: lambda: conv_g(j, 1), 4: lambda: conv_g(j, 0)}

            def val_hooks(j):
                return {2: lambda: conv_val(j, 2), 3: lambda: conv_val(j, 1), 4: lambda: conv_val(j, 0),
                        5: lambda: gated(j)}

            chunk(Q_UP, {3: lambda: rows_lo(1, N4 - 1), 4: rms_2, 6: lambda: inverse(1)})
            with links.loop(0, UP_PAIRS - 1, 4) as j:
                chunk(Q_UP + 1 + j * 2, g_hooks(j))
                chunk(Q_UP + 2 + j * 2, val_hooks(j))
            chunk(Q_DOWN - 1, g_hooks(UP_PAIRS - 1))

            def ff_lo(kt, s, n):
                dve.wait_ge(ff_hi_ready, n)
                nc.vector.tensor_tensor(B_lo[:, s:s + 1, :], ff[:, ds(kt, 1), :], B_hi[:, s:s + 1, :].bitcast(F32),
                                        ALU.subtract).then_inc(ff_lo_ready, 1)

            for n in range(4):
                ff_lo(n, n, n + 1)

            def down(it, hooks={}, last=False):
                for i in range(PIECE_LEAD if last else PIECES):
                    if i in hooks:
                        hooks[i]()
                    split_lo(Q_DOWN + it, i)
                    if i >= 4:
                        ff_lo(it * 4 + i, i - 4, it * 4 + i + 1)

            down(0, {2: lambda: (conv_val(UP_PAIRS - 1, 2), conv_val(UP_PAIRS - 1, 1)),
                     3: lambda: (conv_val(UP_PAIRS - 1, 0), gated(UP_PAIRS - 1))})
            with dve.Fori(1, N_DOWN - 1) as it:
                down(it)
            down(N_DOWN - 1, last=True)
            for n in range(N4):
                for t in range(TT):
                    done = Q_END * PIECES - (4 if n < 2 else 0)
                    if n % 2 and t == TT - 1:
                        dve.wait_ge(piece_used, done)
                    else:
                        dve.wait_ge(bank_done, n // 2 * 3 + n % 2 * TT + t + 1)
                    cols = slice(n * COLS, (n + 1) * COLS)
                    nc.vector.tensor_tensor(xres[:, t, cols], xres[:, t, cols], ps[:, DOWN_BANKS[n][t], :],
                                            ALU.add).then_inc(y_ready, 1)

        @block.tensor
        def _(pe):
            def piece(q, i, par, stat, first, last):
                s = i % PIECE_LEAD
                pe.wait_ge(lo_ready, q * PIECES + i + 1)
                for r in range(2):
                    k = 2 * i + r
                    hi, lo = w_hi[:, s, r * COLS:(r + 1) * COLS], w_lo[:, s, r * COLS:(r + 1) * COLS]
                    for t in range(TT):
                        o = ps[:, 2 * par + t, :]
                        a_hi, a_lo = (a[:, k, t * P:(t + 1) * P] for a in stat)
                        pe.matmul(o, a_hi, hi, start=(first and r == 0), stop=False)
                        pe.matmul(o, a_hi, lo, start=False, stop=False)
                        ins = pe.matmul(o, a_lo, hi, start=False, stop=(last and r == 1))
                ins.then_inc(piece_used, 1)

            def chunk(c, j, stat, hooks={}):
                if not (isinstance(j, int) and c + 2 * j < 2):
                    pe.wait_ge(evacuated[c % 2], j + c // 2)
                for i in range(PIECES):
                    if i in hooks:
                        hooks[i]()
                    piece(c + j * 2, i, c % 2, stat, i == 0, i == PIECES - 1)

            def aux_free(b, uses):
                if not (isinstance(uses, int) and uses == 0):
                    pe.wait_ge(aux_drained[b], uses)

            def transpose_rows(b, uses, src, m=4):
                aux_free(b, uses)
                for n in range(m):
                    for t in range(TT):
                        last = pe.transpose(aux_tiles(b)[:, n, t * P:(t + 1) * P], src[:, t, n * P:(n + 1) * P], ident[:])
                last.then_inc(aux_written[b], 1)

            def parameters():
                pe.wait_ge(params_landed, 10 * 16)
                aux_free(0, AUX0_PARAMS)
                for m in range(KT):
                    pe.transpose(ps[:, 4, m * 32:m * 32 + TAPS], rows_dw[:, m * P:(m + 1) * P], ident[0:TAPS, 0:TAPS])
                pe.transpose(ps[:, 5, 0:NVEC], rows_vec, ident[0:NVEC, 0:NVEC])
                for k in range(3):
                    last = pe.transpose(ps[:, 5, P + k * 2 * FT:P + (k + 1) * 2 * FT], rows_ffn[:, k, :],
                                        ident[0:2 * FT, 0:2 * FT])
                last.then_inc(aux_written[0], 1)

            def rows_in(n, base, c):
                pe.wait_ge(scaled_ready, 4 * n + c + 1)
                transpose_rows(c % 2, base + c // 2, scaled[c % 2])

            def rows_split(base, c):
                pe.wait_ge(aux_drained[c % 2], base + c // 2 + 1)

            A, B = (A_hi, A_lo), (B_hi, B_lo)
            pe.wait_ge(consts_ready, 1)
            rows_in(0, AUX_NORM1, 0)
            rows_in(0, AUX_NORM1, 1)

            def glu_in(j):
                pe.wait_ge(glu_ready, j + 1)
                transpose_rows(0, j + AUX0_GLU, stage2)

            chunk(Q_U, 0, A, {0: lambda: rows_split(AUX_NORM1, 0), 1: lambda: rows_in(0, AUX_NORM1, 2),
                              2: lambda: rows_split(AUX_NORM1, 1), 3: lambda: rows_in(0, AUX_NORM1, 3),
                              4: lambda: rows_split(AUX_NORM1, 2), 6: lambda: rows_split(AUX_NORM1, 3),
                              7: parameters})
            chunk(Q_U + 1, 0, A)
            chunk(Q_U + 2, 0, A, {2: lambda: glu_in(0)})
            with pe.Fori(1, N4 - 1) as j:
                chunk(Q_U + 1, j, A)
                chunk(Q_U + 2, j, A, {2: lambda: glu_in(j)})
            chunk(Q_KV - 1, 0, A)
            chunk(Q_KV, 0, A, {2: lambda: glu_in(N4 - 1)})

            def k_in():
                pe.wait_ge(k_ready, 1)
                aux_free(1, AUX1_KV)
                for g in range(KV_HEADS):
                    for t in range(TT):
                        last = pe.transpose(aux_tiles(1)[:, g, t * P:(t + 1) * P], stage2[:, t, g * P:(g + 1) * P],
                                            ident[:])
                last.then_inc(aux_written[1], 1)

            chunk(Q_Q0, 0, A, {5: k_in})

            def q_in(j):
                pe.wait_ge(qn_ready, j + 1)
                transpose_rows(1, j * 4 + AUX1_ATT, stage2)

            def scores(j, e):
                if e == 0:
                    pe.wait_ge(aux_drained[1], j * 4 + AUX1_ATT + 1)
                aux_free(e, (j * 3 + AUX0_ATT, j * 4 + AUX1_ATT + 1)[e])
                pe.transpose(ps[:, 4 + 2 * e, 0:P], ident[:], ident[:])
                for n in range(4):
                    pair, half = 2 * e + n // 2, 64 * (n % 2)
                    for c in range(NCHUNK):
                        rows = slice(64 * (c % 2), 64 * (c % 2) + 64)
                        cols = (n // 2) * 256 + (c // 2) * P
                        last = pe.matmul(ps[rows, 4 + 2 * e + n % 2, cols:cols + P],
                                         q_t[half:half + 64, pair, c * CHUNK:(c + 1) * CHUNK],
                                         k_head[half:half + 64, c * CHUNK:c * CHUNK + P], start=True, stop=True)
                last.then_inc(aux_written[e], 1)

            def probs_in(j, e):
                pe.wait_ge(prob_ready, j * 2 + e + 1)
                aux_free(0, j * 3 + AUX0_ATT + 1 + e)
                p = (prob0, prob1)[e]
                for n in range(8):
                    last = pe.transpose(aux(0).rearrange("p b n -> p (b n)")[:, n * P:(n + 1) * P],
                                        p[:, n * P:(n + 1) * P], ident[:])
                last.then_inc(aux_written[0], 1)

            def values(j, e):
                pe.wait_ge(aux_drained[0], j * 3 + AUX0_ATT + 2 + e)
                aux_free(1, j * 4 + AUX1_ATT + 2 + e)
                for n in range(4):
                    half, at = 64 * (n % 2), score_place(n) * 256
                    for c in range(NCHUNK):
                        cols = (n // 2) * SEQ + c * CHUNK
                        last = pe.matmul(ps[half:half + 64, 6, cols:cols + CHUNK], v_head[:, c, :],
                                         prob_t[:, at + c * CHUNK:at + (c + 1) * CHUNK],
                                         start=True, stop=True)
                last.then_inc(aux_written[1], 1)

            def att_hooks(j):
                return ({5: lambda: q_in(j), 6: lambda: scores(j, 0), 7: lambda: scores(j, 1)},
                        {3: lambda: probs_in(j, 0), 4: lambda: values(j, 0),
                         5: lambda: probs_in(j, 1), 7: lambda: values(j, 1)})

            with pe.Fori(0, N4 - 1) as j:
                first, second = att_hooks(j)
                chunk(Q_ATT, j, A, first)
                chunk(Q_ATT + 1, j, A, second)
            first, second = att_hooks(N4 - 1)
            chunk(Q_AP - 2, 0, A, first)
            chunk(Q_AP - 1, 0, A, second)

            some, rest = (lambda: pe.wait_ge(aux_drained[1], AUX1_LN - 4)), (lambda: pe.wait_ge(aux_drained[1], AUX1_LN))
            with pe.Fori(0, N4 - 1) as j:
                chunk(Q_AP, j, B, {0: some, 6: rest})
                chunk(Q_AP + 1, j, A)

            def channel_mean(dst, src, m):
                return pe.matmul(dst, mean_of[:], src, start=(m == 0), stop=(m == KT - 1))

            def ln_mean(m0, m1):
                if m0 == 0:
                    pe.wait_ge(consts_done, 1)
                    aux_free(0, AUX0_LN)
                pe.wait_ge(conv_tap, 32 * m1)
                for m in range(m0, m1):
                    last = channel_mean(ps[:, 4, 0:SEQ], glu[:, m, PAD:], m)
                if m1 == KT:
                    last.then_inc(aux_written[0], 1)

            def ln_var(c0, c1):
                for c in range(c0, c1):
                    pe.wait_ge(squared, c + 1)
                    for m in range(4 * c, 4 * c + 4):
                        last = channel_mean(ps[:, 6, 0:SEQ], squares[:, m, :], m)
                if c1 == 4:
                    last.then_inc(aux_written[1], 1)

            chunk(Q_CP - 1, 0, B, {0: lambda: ln_mean(0, KT - 2), 1: lambda: ln_mean(KT - 2, KT),
                                   4: lambda: ln_var(0, 2), 5: lambda: ln_var(2, 4)})

            def mix_in(c):
                pe.wait_ge(mix_ready, c + 1)
                transpose_rows(c % 2, AUX_MIX + c // 2, mix_n)

            for c in range(N4):
                hooks = {2: lambda: mix_in(c - 1)} if c else {2 * g: (lambda g=g: pe.wait_ge(conv_lo, g + 1))
                                                             for g in range(4)}
                chunk(Q_CP + c, 0, A, hooks)

            def mixed(c):
                pe.wait_ge(aux_drained[c % 2], AUX_MIX + c // 2 + 1)

            mixed(0), mixed(1), mixed(2)
            chunk(Q_OUT, 0, B, {1: lambda: mix_in(N4 - 1), 6: lambda: mixed(N4 - 1)})
            for c in range(1, N4):
                chunk(Q_OUT + c, 0, B, {2: lambda: rows_in(1, AUX_NORM2, c - 1)})

            def up_in(b, uses, c, j=0):
                left_psum(pe, c, j)
                transpose_rows(b, uses, up_n)

            for c in range(3):
                rows_split(AUX_NORM2, c)
            chunk(Q_UP, 0, A, {2: lambda: rows_in(1, AUX_NORM2, 3), 6: lambda: rows_split(AUX_NORM2, 3)})
            with pe.Fori(0, UP_PAIRS - 1) as j:
                chunk(Q_UP + 1, j, A, {1: lambda: up_in(0, j + AUX_UP, Q_UP, j)})
                chunk(Q_UP + 2, j, A, {1: lambda: up_in(1, j + AUX_UP, Q_UP + 1, j)})
            chunk(Q_DOWN - 1, 0, A, {1: lambda: up_in(0, AUX_UP + UP_PAIRS - 1, Q_DOWN - 2)})

            left_psum(pe, Q_DOWN - 2)
            aux_free(0, AUX_UP + UP_PAIRS)

            def last_val():
                up_in(1, AUX_UP + UP_PAIRS - 1, Q_DOWN - 1)

            def right_banks():
                left_psum(pe, Q_DOWN - 1)
                aux_free(1, AUX_UP + UP_PAIRS)

            def down(it, hooks={}, first=False, last=False):
                for i in range(PIECES):
                    if i in hooks:
                        hooks[i]()
                    s = i % PIECE_LEAD
                    pe.wait_ge(lo_ready, (Q_DOWN + it) * PIECES + i + 1)
                    kt, half = i % 4, i // 4
                    if half == 0:
                        pe.wait_ge(ff_lo_ready, it * 4 + kt + 1)
                    starts, stops = first and kt == 0, last and kt == 3
                    for r in range(2):
                        n = 2 * half + r
                        hi, lo = w_hi[:, s, r * COLS:(r + 1) * COLS], w_lo[:, s, r * COLS:(r + 1) * COLS]
                        for t in range(TT):
                            o = ps[:, DOWN_BANKS[n][t], :]
                            a_hi, a_lo = (a[:, kt, t * P:(t + 1) * P] for a in B)
                            pe.matmul(o, a_hi, hi, start=starts, stop=False)
                            pe.matmul(o, a_hi, lo, start=False, stop=False)
                            ins = pe.matmul(o, a_lo, hi, start=False, stop=stops)
                            if stops and not (r == 1 and t == TT - 1):
                                ins.then_inc(bank_done, 1)
                    ins.then_inc(piece_used, 1)

            down(0, {1: last_val, 4: right_banks}, first=True)
            with pe.Fori(1, N_DOWN - 1) as it:
                down(it)
            down(N_DOWN - 1, last=True)


_INS = ['x', 'norm_mix_g', 'w_in', 'q_norm_g', 'k_norm_g', 'sinks', 'w_attn_proj', 'conv_dw_w', 'conv_dw_b',
        'conv_ln_g', 'conv_ln_b', 'w_conv_proj', 'w_out', 'norm_ffn_g', 'w_up', 'ffn_dw_w', 'w_down']
_OUTS = [((1, 256, 2048), 'float32')]


def kernel(**inputs):
    import numpy as _np
    import concourse.bacc as _bacc
    from concourse import mybir as _mybir
    from concourse.bass_utils import run_bass_kernel_spmd as _run

    nc = _bacc.Bacc("TRN2", target_bir_lowering=False, num_devices=1)
    arrays, args = {}, []
    for name in _INS:
        a = _np.ascontiguousarray(inputs[name])
        arrays[f"in_{name}_dram"] = a
        args.append(nc.dram_tensor(f"in_{name}_dram", a.shape, _mybir.dt.from_np(a.dtype), kind="ExternalInput").ap())
    for i, (shape, dtype) in enumerate(_OUTS):
        dt = _mybir.dt.from_np(_np.dtype(dtype))
        args.append(nc.dram_tensor(f"out_{i}_dram", shape, dt, kind="ExternalOutput").ap())
    trunk(nc, *args)
    r = _run(nc, [arrays], core_ids=[0])
    got = tuple(r.results[0][f"out_{i}_dram"] for i in range(len(_OUTS)))
    return got[0]
```

```python
from contextlib import ExitStack, contextmanager

import concourse.bass as bass
from concourse import mybir

ACT = mybir.ActivationFunctionType
ALU = mybir.AluOpType
AX_X = mybir.AxisListType.X
F32 = mybir.dt.float32
F32R = mybir.dt.float32r
ds = bass.ds

P = 128
D = 2048
SEQ = 256
TT = SEQ // P
KT = D // P
COLS = 512
HEADS, KV_HEADS, HD = 32, 4, 64
GROUP = HEADS // KV_HEADS
CHUNK = 64
NCHUNK = SEQ // CHUNK
TAPS = 31
PAD = TAPS - 1
STEPS = TAPS + 1
EARLY_STEPS = STEPS - 2
EARLY = 10
LATE = 11
FF = 5632
FT = FF // P
UP_PAIRS = FF // COLS
EPS = 1e-6
KV_W = KV_HEADS * HD

PIECES = 8
PIECE_LEAD = 4
N4 = D // COLS

COL_Q, COL_KV = 0, D
COL_A = D + 2 * KV_W
COL_GLU = COL_A + D
COL_GATE_A = COL_GLU + D
COL_GATE_B = COL_GATE_A + D

Q_U = 0
Q_KV = Q_U + 2 * N4
Q_Q0 = Q_KV + 1
Q_ATT = Q_Q0 + 1
Q_AP = Q_ATT + 2 * N4
Q_CP = Q_AP + 2 * N4 - 1
Q_OUT = Q_CP + N4
Q_UP = Q_OUT + N4
Q_DOWN = Q_UP + 2 * UP_PAIRS
N_DOWN = FT // 4
Q_END = Q_DOWN + N_DOWN

AUX_NORM1 = 0
AUX0_PARAMS = 2
AUX0_GLU = 3
AUX1_KV = 2
AUX0_ATT, AUX1_ATT = AUX0_GLU + N4, AUX1_KV + 1
AUX0_LN, AUX1_LN = AUX0_ATT + 3 * N4, AUX1_ATT + 4 * N4
AUX_MIX = AUX0_LN + 1
AUX_NORM2 = AUX_MIX + 2
AUX_UP = AUX_NORM2 + 2
assert AUX0_LN == AUX1_LN

ALL_CONV_STEPS = LATE * EARLY_STEPS + (KT - LATE) * STEPS
LN_PARTS = ((0, 4), (4, 8), (8, LATE), (LATE, KT))

DOWN_BANKS = ((2, 3), (4, 5), (0, 1), (6, 7))

V_DWB, V_LNG, V_LNB = 0, KT, 2 * KT
V_QG = 3 * KT
V_KG = V_QG + 1
NVEC = V_KG + 1


def score_place(n):
    return 2 * (n % 2) + n // 2


class Chain:

    def __init__(self, eng, sem):
        self.eng, self.sem, self.at, self.shift = eng, sem, 0, 0

    def link(self, ins):
        ins.then_inc(self.sem, 1)
        self.at += 1
        self.eng.wait_ge(self.sem, self.at + self.shift)

    @contextmanager
    def loop(self, first, end, per_trip):
        start = self.at
        with self.eng.Fori(first, end) as j:
            self.shift = (j - first) * per_trip
            yield j
        assert self.at - start == per_trip, (self.at - start, per_trip)
        self.at = start + per_trip * (end - first)
        self.shift = 0


def trunk(nc, x, norm_mix_g, w_in, q_norm_g, k_norm_g, sinks, w_attn_proj, conv_dw_w, conv_dw_b,
          conv_ln_g, conv_ln_b, w_conv_proj, w_out, norm_ffn_g, w_up, ffn_dw_w, w_down, out):
    ctx = ExitStack()
    with ctx:
        def sb(name, shape, dt=F32):
            return ctx.enter_context(nc.sbuf_tensor(name, shape, dt))

        def sem(name):
            return ctx.enter_context(nc.semaphore(name))

        raw = sb("raw", [P, PIECE_LEAD, 1024])
        w_hi = sb("w_hi", [P, PIECE_LEAD, 1024], F32R)
        w_lo = sb("w_lo", [P, PIECE_LEAD, 1024], F32R)
        A_hi, A_lo = sb("A_hi", [P, KT, SEQ], F32R), sb("A_lo", [P, KT, SEQ], F32R)
        B_hi, B_lo = sb("B_hi", [P, KT, SEQ], F32R), sb("B_lo", [P, KT, SEQ], F32R)
        xres = sb("xres", [P, TT, D])
        big = sb("big", [P, 2 * TT * D + KT * (PAD + SEQ)])
        gates_a = big[:, 0:TT * D].rearrange("p (t n) -> p t n", t=TT)
        gates_b = big[:, TT * D:2 * TT * D].rearrange("p (t n) -> p t n", t=TT)
        glu = big[:, 2 * TT * D:].rearrange("p (m t) -> p m t", m=KT)
        ff = big[:, 0:FT * SEQ].rearrange("p (m t) -> p m t", m=FT)
        flat = xres[:, :, :].rearrange("p t n -> p (t n)")
        stage1 = flat[:, 0:1024].rearrange("p (t n) -> p t n", t=TT)
        stage2 = flat[:, 1024:2048].rearrange("p (t n) -> p t n", t=TT)
        stage3 = flat[:, 2048:3072].rearrange("p (t n) -> p t n", t=TT)
        q_t = flat[:, 2048:3072].rearrange("p (m t) -> p m t", m=4)
        prob0 = flat[:, 3072:4096]
        squares = flat.rearrange("p (m t) -> p m t", m=KT)
        work1 = sb("work1", [P, 1024])
        work2 = sb("work2", [P, 1024])
        work3 = sb("work3", [P, 1024])
        prob1 = work1[:, :]
        prob_t = work2[:, :]
        v_band = work3[:, :].rearrange("p (c n) -> p c n", c=NCHUNK)
        scaled = [work1[:, :].rearrange("p (t n) -> p t n", t=TT), work2[:, :].rearrange("p (t n) -> p t n", t=TT)]
        mix_n = scaled[0]
        up_n = scaled[0]
        g_t = work2[:, :].rearrange("p (m t) -> p m t", m=4)
        val_t = work3[:, :].rearrange("p (m t) -> p m t", m=4)
        last_val = work1[:, :].rearrange("p (m t) -> p m t", m=4)
        k_t = sb("k_t", [P, KV_HEADS, CHUNK + SEQ])
        k_head = sb("k_head", [P, CHUNK + SEQ])
        v_head = sb("v_head", [P, NCHUNK, HD])
        dist = sb("dist", [P, TT, P])
        conv_acc = sb("conv_acc", [P, 2, 2, SEQ])
        dist_raw = conv_acc[:, 0, :, :].rearrange("p a t -> p (a t)")[:, 0:TT * P]
        early_mean = k_head[:, 0:SEQ]
        rest_mean, mean_sq = conv_acc[:, 0, 0, :], conv_acc[:, 0, 1, :]
        conv_var, conv_sd, conv_r = conv_acc[:, 1, 0, :], conv_acc[:, 1, 1, :], conv_acc[:, 0, 1, :]
        dw_t = sb("dw_t", [P, KT, TAPS])
        vecs = sb("vecs", [P, NVEC])
        q_gain = sb("q_gain", [P, 1])
        ffn_dw = sb("ffn_dw", [P, 3, 2 * FT])
        neg_slope = sb("neg_slope", [P, HEADS])
        sink_rows = sb("sink_rows", [P, HEADS])
        sink = sb("sink", [P, HEADS])
        ident = sb("ident", [P, P])
        mean_of = sb("mean_of", [P, P])
        stats = sb("stats", [P, 81])
        rms_ms, rms_sd, rms_r, ssq_all = (stats[:, 2 * n:2 * n + 2] for n in range(4))
        ssq = stats[:, 8:16].rearrange("p (t c) -> p t c", t=TT)
        hs_sum, hs_ms, hs_sd, hs_r = (stats[:, 16 + 16 * n:32 + 16 * n] for n in range(4))
        soft = sb("soft", [P, 2, 6, 8])

        ps = ctx.enter_context(nc.psum_tensor("ps", [P, 8, COLS], F32))

        def acc(par):
            return ps[:, 2 * par:2 * par + 2, :]

        def aux(b):
            return ps[:, 4 + 2 * b:6 + 2 * b, :]

        def aux_tiles(b, m=4):
            return aux(b).rearrange("p b n -> p (b n)").rearrange("p (m t) -> p m t", m=m)

        rows_dw = big[0:TAPS, 0:D]
        rows_vec = big[0:NVEC, D:D + P]
        rows_ffn = big[0:2 * FT, D + P:D + 4 * P].rearrange("p (k n) -> p k n", k=3)
        junk = gates_b
        gain = big[:, 2 * TT * D:2 * TT * D + D]

        raw_landed = [sem(f"raw_landed{i}") for i in range(PIECE_LEAD)]
        hi_ready, lo_ready, piece_used = sem("hi_ready"), sem("lo_ready"), sem("piece_used")
        evacuated = [sem("evacuated_even"), sem("evacuated_odd")]
        aux_written = [sem("aux_written0"), sem("aux_written1")]
        aux_drained = [sem("aux_drained0"), sem("aux_drained1")]
        x_landed = [sem(f"x_landed{c}") for c in range(N4)]
        gain0_landed, gain_landed, params_landed, x_reloaded = (sem(n) for n in (
            "gain0_landed", "gain_landed", "params_landed", "x_reloaded"))
        consts_ready, iota_ready, consts_done = sem("consts_ready"), sem("iota_ready"), sem("consts_done")
        pool_step = sem("pool_step")
        dve_step = sem("dve_step")
        ssq_ready, ms_ready, sd_ready, rms_ready, scaled_ready, scaled_hi = (sem(n) for n in (
            "ssq_ready", "ms_ready", "sd_ready", "rms_ready", "scaled_ready", "scaled_hi"))
        glu_ready = sem("glu_ready")
        k_ready, v_shifted = sem("k_ready"), sem("v_shifted")
        hs_squared, hs_ms_ready, hs_sd_ready, qn_ready = (sem(n) for n in (
            "hs_squared", "hs_ms_ready", "hs_sd_ready", "qn_ready"))
        max_ready, exp_ready, prob_ready, o_hi_ready = (sem(n) for n in (
            "max_ready", "exp_ready", "prob_ready", "o_hi_ready"))
        conv_started, conv_tap = sem("conv_started"), sem("conv_tap")
        early_mean_written, early_mean_ready = sem("early_mean_written"), sem("early_mean_ready")
        centred, squared, var_sd, ln_scaled, ln_silu, conv_hi, conv_lo = (sem(n) for n in (
            "centred", "squared", "var_sd", "ln_scaled", "ln_silu", "conv_hi", "conv_lo"))
        mix_ready, mix_hi = sem("mix_ready"), sem("mix_hi")
        g_silu, ff_ready = sem("g_silu"), sem("ff_ready")
        ff_hi_ready, ff_lo_ready = sem("ff_hi_ready"), sem("ff_lo_ready")
        bank_done, y_ready, stored = sem("bank_done"), sem("y_ready"), sem("stored")

        block = ctx.enter_context(nc.Block())

        def left_psum(eng, c, j=0):
            eng.wait_ge(evacuated[c % 2], j + (c // 2 + 1))

        @block.sync
        def _(sp):
            x_rows = x[0].rearrange("(t p) n -> p t n", p=P)

            def load_x(c):
                cols = slice(c * COLS, (c + 1) * COLS)
                sp.dma_start(xres[:, :, cols], x_rows[:, :, cols]).then_inc(x_landed[c], 16)

            def load_gain(c0, c1, landed):
                sp.dma_start(gain[:, c0:c1], norm_mix_g[:, c0:c1].partition_broadcast(P)).then_inc(landed, 16)

            load_x(0)
            load_gain(0, COLS, gain0_landed)

            def load_parameters():
                for n, v in enumerate((conv_dw_b, conv_ln_g, conv_ln_b)):
                    sp.dma_start(rows_vec[n * KT:(n + 1) * KT, :],
                                 v[0].rearrange("(m n) -> m n", n=P)).then_inc(params_landed, 16)
                for n, v in enumerate((q_norm_g, k_norm_g)):
                    for half in range(2):
                        sp.dma_start(rows_vec[V_QG + n:V_QG + n + 1, half * HD:(half + 1) * HD],
                                     v).then_inc(params_landed, 16)
                sp.dma_start(rows_dw, conv_dw_w[0]).then_inc(params_landed, 16)
                sp.dma_start(rows_ffn, ffn_dw_w[0].rearrange("k (m n) -> m k n", n=P)).then_inc(params_landed, 16)
                sp.dma_start(sink_rows[:], sinks.partition_broadcast(P)).then_inc(params_landed, 16)

            def load_chunk(q, w, c0, first=0):
                rows = w.rearrange("(i r p) n -> i p r n", r=2, p=P)
                for i in range(PIECES):
                    if first and i == 2:
                        load_gain(COLS, D, gain_landed)
                    if first and i in (2, 4, 6):
                        load_x(i // 2)
                    if first and i == 7:
                        load_parameters()
                    if i >= first:
                        sp.wait_ge(lo_ready, q * PIECES + i - (PIECE_LEAD - 1))
                    sp.dma_start(raw[:, i % PIECE_LEAD, :].rearrange("p (r n) -> p r n", r=2),
                                 rows[i][:, :, ds(c0, COLS)]).then_inc(raw_landed[i % PIECE_LEAD], 16)

            wi = w_in[0]
            load_chunk(Q_U, wi, COL_A, first=PIECE_LEAD)
            with sp.Fori(0, N4 - 1) as j:
                load_chunk(Q_U + 1 + j * 2, wi, COL_GLU + j * COLS)
                load_chunk(Q_U + 2 + j * 2, wi, COL_A + COLS + j * COLS)
            load_chunk(Q_KV - 1, wi, COL_GLU + (N4 - 1) * COLS)
            load_chunk(Q_KV, wi, COL_KV)
            load_chunk(Q_Q0, wi, COL_Q)
            with sp.Fori(0, N4 - 1) as j:
                load_chunk(Q_ATT + j * 2, wi, COL_GATE_A + j * COLS)
                load_chunk(Q_ATT + 1 + j * 2, wi, COL_Q + COLS + j * COLS)
            load_chunk(Q_AP - 2, wi, COL_GATE_A + (N4 - 1) * COLS)
            load_chunk(Q_AP - 1, wi, COL_GATE_B)
            with sp.Fori(0, N4 - 1) as j:
                load_chunk(Q_AP + j * 2, w_attn_proj[0], j * COLS)
                load_chunk(Q_AP + 1 + j * 2, wi, COL_GATE_B + COLS + j * COLS)
            load_chunk(Q_CP - 1, w_attn_proj[0], (N4 - 1) * COLS)
            with sp.Fori(0, N4) as j:
                load_chunk(Q_CP + j, w_conv_proj[0], j * COLS)
            sp.wait_ge(conv_lo, 4)
            sp.dma_start(xres[:], x_rows).then_inc(x_reloaded, 16)
            sp.dma_start(gain, norm_ffn_g.partition_broadcast(P)).then_inc(gain_landed, 16)
            with sp.Fori(0, N4) as j:
                load_chunk(Q_OUT + j, w_out[0], j * COLS)
            with sp.Fori(0, UP_PAIRS) as j:
                load_chunk(Q_UP + j * 2, w_up[0], j * COLS)
                load_chunk(Q_UP + 1 + j * 2, w_up[0], FF + j * COLS)
            down_rows = w_down[0].rearrange("(k p) n -> p k n", p=P)
            with sp.Fori(0, N_DOWN) as it:
                for i in range(PIECES):
                    sp.wait_ge(lo_ready, (Q_DOWN + it) * PIECES + i - (PIECE_LEAD - 1))
                    half = i // 4
                    sp.dma_start(raw[:, i % PIECE_LEAD:i % PIECE_LEAD + 1, :],
                                 down_rows[:, ds(it * 4 + i % 4, 1), half * 1024:(half + 1) * 1024]
                                 ).then_inc(raw_landed[i % PIECE_LEAD], 16)
            dst = out[0].rearrange("(t p) n -> p t n", p=P)
            for n in range(N4):
                for t in range(TT):
                    sp.wait_ge(y_ready, n * TT + t + 1)
                    sp.dma_start(dst[:, t, n * COLS:(n + 1) * COLS],
                                 xres[:, t, n * COLS:(n + 1) * COLS]).then_inc(stored, 16)
            sp.wait_ge(stored, 16 * N4 * TT)

        @block.gpsimd
        def _(pool):
            n = 0

            def step(ins):
                nonlocal n
                ins.then_inc(pool_step, 1)
                n += 1
                pool.wait_ge(pool_step, n)

            step(nc.gpsimd.memset(ident[:], 0.0))
            nc.gpsimd.affine_select(out=ident[:], in_=ident[:], compare_op=ALU.not_equal, fill=1.0, base=0,
                                    pattern=[[-1, P]], channel_multiplier=1).then_inc(consts_ready, 1)
            pool.wait_ge(consts_ready, 1)
            for half in range(2):
                nc.gpsimd.iota(dist_raw[64 * half:64 * half + 64, :].rearrange("p (t s) -> p t s", t=TT),
                               pattern=[[0, TT], [-1, P]], base=CHUNK, channel_multiplier=1,
                               allow_small_or_imprecise_dtypes=True).then_inc(iota_ready, 1)
                pool.wait_ge(iota_ready, half + 1)
            step(nc.gpsimd.memset(mean_of[:], 1.0 / D))
            for h in range(HEADS):
                at = h // 4 * 4 + score_place(h % 4)
                step(nc.gpsimd.memset(neg_slope[:, at:at + 1], -(2.0 ** (-8.0 * (h + 1) / HEADS))))
            nc.gpsimd.memset(k_t[:, :, 0:CHUNK], 0.0).then_inc(consts_done, 1)

        @block.scalar
        def _(act):
            def split_hi(q, i):
                s = i % PIECE_LEAD
                act.wait_ge(raw_landed[s], (q * 2 + 2 + i // PIECE_LEAD) * 16)
                act.wait_ge(piece_used, q * PIECES + i + 1)
                nc.scalar.activation(w_hi[:, s, :], raw[:, s, :], ACT.Copy).then_inc(hi_ready, 1)

            def chunk(q, hooks={}):
                for i in range(PIECES):
                    if i in hooks:
                        hooks[i]()
                    split_hi(q, i)

            def finished(q):
                act.wait_ge(piece_used, (q + 1) * PIECES)

            def rows_hi(base, c):
                act.wait_ge(aux_written[c % 2], base + c // 2 + 1)
                nc.scalar.activation(A_hi[:, 4 * c:4 * c + 4, :], aux_tiles(c % 2), ACT.Copy).then_inc(scaled_hi, 1)

            def root(n):
                act.wait_ge(ms_ready, n + 1)
                nc.scalar.activation(rms_sd, rms_ms, ACT.Sqrt).then_inc(sd_ready, 1)

            act.wait_ge(consts_ready, 1)
            nc.scalar.activation(stats[:, 80:81], ident[:, 0:1], ACT.Copy)

            for i in range(PIECE_LEAD):
                act.wait_ge(raw_landed[i], 16)
                nc.scalar.activation(w_hi[:, i, :], raw[:, i, :], ACT.Copy).then_inc(hi_ready, 1)
                if i % 2 == 0:
                    rows_hi(AUX_NORM1, i // 2)

            def squares_of(c):
                cols = slice(c * COLS, (c + 1) * COLS)
                for t in range(TT):
                    nc.scalar.activation(junk[:, t, cols], xres[:, t, cols], ACT.Square,
                                         accum_out=ssq[:, t, c:c + 1]).then_inc(ssq_ready, 1)

            def square_x(c):
                act.wait_ge(x_landed[c], 16)
                squares_of(c)

            def glu_out(j):
                act.wait_ge(aux_written[0], AUX0_GLU + 1 + j)
                nc.scalar.activation(glu[:, ds(j * 4, 4), PAD:], aux_tiles(0), ACT.Copy).then_inc(aux_drained[0], 1)

            def conv_start(m, buf, free_after=None):
                if free_after is not None:
                    act.wait_ge(conv_tap, free_after * EARLY_STEPS + EARLY_STEPS)
                tile = glu[:, ds(m, 1), :].rearrange("p m t -> p (m t)")
                w0, w1 = (dw_t[:, ds(m, 1), k:k + 1].rearrange("p m k -> p (m k)") for k in range(2))
                nc.scalar.activation(conv_acc[:, buf, 0, :], tile[:, 0:SEQ], ACT.Identity, scale=w0,
                                     bias=vecs[:, ds(m + V_DWB, 1)]).then_inc(conv_started, 1)
                nc.scalar.activation(conv_acc[:, buf, 1, :], tile[:, 1:1 + SEQ], ACT.Copy,
                                     scale=w1).then_inc(conv_started, 1)

            def evac(c, j, dst, func):
                finished(c + j * 2)
                for t in range(TT):
                    last = nc.scalar.activation(dst[:, t, :], acc(c % 2)[:, t, :], func, scale=rms_r[:, t:t + 1])
                last.then_inc(evacuated[c % 2], 1)

            def square_heads(c, j, width):
                left_psum(act, c, j)
                nc.scalar.activation(stage3[:, :, 0:width], stage1[:, :, 0:width], ACT.Square).then_inc(hs_squared, 1)

            chunk(Q_U, {0: lambda: square_x(0), 2: lambda: square_x(1), 3: lambda: rows_hi(AUX_NORM1, 2),
                        4: lambda: square_x(2), 5: lambda: rows_hi(AUX_NORM1, 3), 6: lambda: square_x(3)})
            root(0)
            act.wait_ge(rms_ready, 1)
            evac(Q_U, 0, stage1, ACT.Copy)
            chunk(Q_U + 1)
            evac(Q_U + 1, 0, stage3, ACT.Sigmoid)

            def first_convs():
                glu_out(0)
                act.wait_ge(aux_drained[0], AUX0_GLU + 1)
                conv_start(0, 0)
                conv_start(1, 1)

            chunk(Q_U + 2, {4: first_convs})
            evac(Q_U + 2, 0, stage1, ACT.Copy)
            with act.Fori(1, N4 - 1) as j:
                chunk(Q_U + 1 + j * 2, {6: lambda: conv_start(j * 2, 0, j * 2 - 2)})
                evac(Q_U + 1, j, stage3, ACT.Sigmoid)
                chunk(Q_U + 2 + j * 2, {4: lambda: glu_out(j), 6: lambda: conv_start(j * 2 + 1, 1, j * 2 - 1)})
                evac(Q_U + 2, j, stage1, ACT.Copy)
            chunk(Q_KV - 1)
            evac(Q_KV - 1, 0, stage3, ACT.Sigmoid)
            chunk(Q_KV, {1: lambda: conv_start(6, 0, 4), 4: lambda: glu_out(N4 - 1)})
            evac(Q_KV, 0, stage1, ACT.Copy)
            square_heads(Q_KV, 0, KV_W)

            act.dma_start(v_band[64:P, 0, :], stage1[0:64, 0, KV_W:]).then_inc(v_shifted, 16)
            act.dma_start(v_band[0:64, 2, :], stage1[64:P, 0, KV_W:]).then_inc(v_shifted, 16)
            act.dma_start(v_band[64:P, 2, :], stage1[0:64, 1, KV_W:]).then_inc(v_shifted, 16)

            def head_root(n):
                act.wait_ge(hs_ms_ready, n + 1)
                nc.scalar.activation(hs_sd, hs_ms, ACT.Sqrt).then_inc(hs_sd_ready, 1)

            def k_out():
                act.wait_ge(aux_written[1], AUX1_KV + 1)
                nc.scalar.activation(k_t[:, :, CHUNK:], aux_tiles(1), ACT.Copy,
                                     scale=vecs[:, V_KG:V_KG + 1]).then_inc(aux_drained[1], 1)
                act.wait_ge(v_shifted, 48)

            chunk(Q_Q0, {1: lambda: head_root(0), 3: lambda: conv_start(7, 1, 5), 5: k_out})
            evac(Q_Q0, 0, stage1, ACT.Copy)
            square_heads(Q_Q0, 0, COLS)

            def q_out(j):
                act.wait_ge(aux_written[1], AUX1_ATT + 1 + j * 4)
                nc.scalar.activation(q_t, aux_tiles(1), ACT.Copy, scale=q_gain[:]).then_inc(aux_drained[1], 1)

            def exps(j, e):
                act.wait_ge(max_ready, j * 2 + e + 1)
                p = (prob0, prob1)[e]
                s = soft[:, e]
                for n in range(8):
                    nc.scalar.activation(p[:, n * P:(n + 1) * P], p[:, n * P:(n + 1) * P], ACT.Exp,
                                         bias=s[:, 1, n:n + 1], accum_out=s[:, 3, n:n + 1])
                nc.scalar.activation(s[:, 4, :], s[:, 2, :], ACT.Exp).then_inc(exp_ready, 1)

            def prob_out(j, e):
                act.wait_ge(aux_written[0], AUX0_ATT + 2 + e + j * 3)
                nc.scalar.activation(prob_t, aux(0).rearrange("p b n -> p (b n)"), ACT.Copy).then_inc(aux_drained[0], 1)

            def o_out(j, e):
                act.wait_ge(aux_written[1], AUX1_ATT + 3 + e + j * 4)
                nc.scalar.activation(B_hi[:, ds(j * 4 + 2 * e, 2), :], aux_tiles(1)[:, 2 * e:2 * e + 2, :],
                                     ACT.Copy).then_inc(o_hi_ready, 1)

            def next_conv(j):
                if not isinstance(j, int):
                    conv_start(j + 8, 1, j + 7)

            def att_hooks(j):
                return ({1: lambda: head_root(j + 1), 5: lambda: q_out(j), 7: lambda: exps(j, 0)},
                        {1: lambda: exps(j, 1),
                         2: lambda: evac(Q_ATT, j, gates_a[:, :, ds(j * COLS, COLS)], ACT.Sigmoid),
                         4: lambda: prob_out(j, 0), 6: lambda: (prob_out(j, 1), o_out(j, 0)),
                         7: lambda: (next_conv(j), o_out(j, 1))})

            with act.Fori(0, N4 - 1) as j:
                first, second = att_hooks(j)
                chunk(Q_ATT + j * 2, first)
                chunk(Q_ATT + 1 + j * 2, second)
                evac(Q_ATT + 1, j, stage1, ACT.Copy)
                square_heads(Q_ATT + 1, j, COLS)
            first, second = att_hooks(N4 - 1)
            chunk(Q_AP - 2, first)
            chunk(Q_AP - 1, second)
            evac(Q_AP - 1, 0, gates_b[:, :, 0:COLS], ACT.Sigmoid)

            def ln_squares(c, m0, m1):
                if m1 <= LATE:
                    act.wait_ge(centred, c + 1)
                else:
                    act.wait_ge(conv_tap, ALL_CONV_STEPS)
                nc.scalar.activation(squares[:, m0:m1, :], glu[:, m0:m1, PAD:], ACT.Square).then_inc(squared, 1)

            def gate_b_out(n):
                evac(Q_AP + 1, n, gates_b[:, :, (n + 1) * COLS:(n + 2) * COLS], ACT.Sigmoid)

            def ln_root():
                act.wait_ge(aux_drained[1], AUX1_LN + 1)
                nc.scalar.activation(conv_sd, conv_var, ACT.Sqrt).then_inc(var_sd, 1)

            chunk(Q_AP)
            chunk(Q_AP + 1)
            gate_b_out(0)
            chunk(Q_AP + 2, {0: lambda: ln_squares(0, *LN_PARTS[0])})
            chunk(Q_AP + 3)
            gate_b_out(1)
            chunk(Q_AP + 4)
            chunk(Q_AP + 5, {1: lambda: ln_squares(1, *LN_PARTS[1]), 4: lambda: ln_squares(2, *LN_PARTS[2]),
                             5: lambda: ln_squares(3, *LN_PARTS[3])})
            gate_b_out(2)

            def ln_swish(c):
                act.wait_ge(ln_scaled, c + 1)
                for m in range(4 * c, 4 * c + 4):
                    last = nc.scalar.activation(glu[:, m, PAD:], glu[:, m, PAD:], ACT.Silu,
                                                scale=vecs[:, V_LNG + m:V_LNG + m + 1],
                                                bias=vecs[:, V_LNB + m:V_LNB + m + 1])
                last.then_inc(ln_silu, 1)
                act.wait_ge(ln_silu, c + 1)
                nc.scalar.activation(A_hi[:, 4 * c:4 * c + 4, :], glu[:, 4 * c:4 * c + 4, PAD:],
                                     ACT.Copy).then_inc(conv_hi, 1)

            chunk(Q_CP - 1, {0: ln_root, 4: lambda: ln_swish(0), 6: lambda: ln_swish(1)})

            def mix_out(c):
                act.wait_ge(aux_written[c % 2], AUX_MIX + c // 2 + 1)
                nc.scalar.activation(B_hi[:, 4 * c:4 * c + 4, :], aux_tiles(c % 2), ACT.Copy).then_inc(mix_hi, 1)

            for c in range(N4):
                chunk(Q_CP + c, {3: lambda: mix_out(c - 1)} if c else
                      {0: lambda: ln_swish(2), 2: lambda: ln_swish(3)})

            def h_out(c):
                rows_hi(AUX_NORM2, c)
                squares_of(c)

            chunk(Q_OUT, {3: lambda: mix_out(N4 - 1)})
            for c in range(1, N4):
                chunk(Q_OUT + c, {2: lambda: h_out(c - 1)})

            def silu_g(j):
                act.wait_ge(aux_drained[0], j + AUX_UP + 1)
                nc.scalar.activation(g_t, g_t, ACT.Silu).then_inc(g_silu, 1)

            chunk(Q_UP, {2: lambda: h_out(N4 - 1), 5: lambda: root(1)})
            act.wait_ge(rms_ready, 2)
            evac(Q_UP, 0, up_n, ACT.Copy)
            with act.Fori(0, UP_PAIRS - 1) as j:
                chunk(Q_UP + 1 + j * 2, {6: lambda: silu_g(j)})
                evac(Q_UP + 1, j, up_n, ACT.Copy)
                chunk(Q_UP + 2 + j * 2)
                evac(Q_UP + 2, j, up_n, ACT.Copy)

            def split_ff(kt, s):
                nc.scalar.activation(B_hi[:, s:s + 1, :], ff[:, ds(kt, 1), :], ACT.Copy).then_inc(ff_hi_ready, 1)

            act.wait_ge(ff_ready, 1)
            chunk(Q_DOWN - 1, {6: lambda: silu_g(UP_PAIRS - 1),
                               **{n: (lambda n=n: split_ff(n, n)) for n in range(4)}})
            evac(Q_DOWN - 1, 0, up_n, ACT.Copy)

            def last_val_out():
                act.wait_ge(aux_written[1], AUX_UP + UP_PAIRS)
                nc.scalar.activation(last_val, aux_tiles(1), ACT.Copy).then_inc(aux_drained[1], 1)

            def down(it, hooks={}, last=False):
                for i in range(PIECE_LEAD if last else PIECES):
                    if i in hooks:
                        hooks[i]()
                    split_hi(Q_DOWN + it, i)
                    if i >= 4:
                        split_ff(it * 4 + i, i - 4)

            down(0, {2: last_val_out})
            act.wait_ge(ff_ready, UP_PAIRS)
            with act.Fori(1, N_DOWN - 1) as it:
                down(it)
            down(N_DOWN - 1, last=True)

        @block.vector
        def _(dve):
            links = Chain(dve, dve_step)
            link = links.link

            def split_lo(q, i):
                s = i % PIECE_LEAD
                dve.wait_ge(hi_ready, q * PIECES + PIECE_LEAD + i + 1)
                nc.vector.tensor_tensor(w_lo[:, s, :], raw[:, s, :], w_hi[:, s, :].bitcast(F32),
                                        ALU.subtract).then_inc(lo_ready, 1)

            def chunk(q, hooks={}, conv={}):
                for part in conv.get(-1, ()):
                    conv_steps(*part)
                for i in range(PIECES):
                    if i in hooks:
                        hooks[i]()
                    split_lo(q, i)
                    for part in conv.get(i, ()):
                        conv_steps(*part)

            def spread(m, buf, k, counts):
                conv = {}
                for i, n in counts.items():
                    conv[i] = [(m, buf, k, k + n)]
                    k += n
                return conv

            def conv_run(done, counts, late):
                conv, per_tile = {}, STEPS if late else EARLY_STEPS
                for i, n in counts.items():
                    conv[i] = []
                    while n:
                        m, k = divmod(done, per_tile)
                        some = min(n, per_tile - k)
                        conv[i].append((LATE + m, 0, k, k + some, 1) if late else (m, m % 2, k + 2, k + 2 + some))
                        done, n = done + some, n - some
                return conv

            def conv_steps(m, buf, k0, k1, late=0):
                tile = glu[:, ds(m, 1), :].rearrange("p m t -> p (m t)")
                for k in range(k0, k1):
                    a = conv_acc[:, buf, k % 2, :]
                    before = LATE * EARLY_STEPS + (m - LATE) * STEPS + k if late else m * EARLY_STEPS + k - 2
                    if not late and k in (2, 3):
                        dve.wait_ge(conv_started, m * 2 + k - 1)
                    elif k >= 1:
                        dve.wait_ge(conv_tap, before if k in (1, 30, 31) else before - 1)
                    if k < 31:
                        src = tile[:, k:k + SEQ]
                        w = dw_t[:, ds(m, 1), k:k + 1].rearrange("p m k -> p (m k)")
                    if k == 0:
                        ins = nc.vector.tensor_scalar(a, src, w, vecs[:, ds(m + V_DWB, 1)], ALU.mult, ALU.add)
                    elif k == 1:
                        ins = nc.vector.scalar_tensor_tensor(out=a, in0=src, scalar=w, in1=early_mean,
                                                             op0=ALU.mult, op1=ALU.subtract)
                    elif k < 30:
                        ins = nc.vector.scalar_tensor_tensor(out=a, in0=src, scalar=w, in1=a,
                                                             op0=ALU.mult, op1=ALU.add)
                    elif k == 30:
                        ins = nc.vector.scalar_tensor_tensor(out=tile[:, PAD:], in0=src, scalar=w, in1=a,
                                                             op0=ALU.mult, op1=ALU.add)
                    else:
                        ins = nc.vector.tensor_tensor(tile[:, PAD:], tile[:, PAD:], a, ALU.add)
                    ins.then_inc(conv_tap, 1)

            CONV_STEPS = {-1: 4, 0: 3, 1: 3, 2: 4, 3: 3, 4: 4, 5: 4, 6: 3}
            per_chunk = sum(CONV_STEPS.values())

            def scale_rows(c):
                cols = slice(c * COLS, (c + 1) * COLS)
                nc.vector.tensor_tensor(scaled[c % 2], xres[:, :, cols],
                                        gain[:, cols].unsqueeze(1).to_broadcast([P, TT, COLS]),
                                        ALU.mult).then_inc(scaled_ready, 1)

            def rows_lo(n, c):
                dve.wait_ge(scaled_hi, 4 * n + c + 1)
                nc.vector.tensor_tensor(A_lo[:, 4 * c:4 * c + 4, :], aux_tiles(c % 2),
                                        A_hi[:, 4 * c:4 * c + 4, :].bitcast(F32),
                                        ALU.subtract).then_inc(aux_drained[c % 2], 1)

            def inverse(n):
                dve.wait_ge(sd_ready, n + 1)
                nc.vector.reciprocal(rms_r, rms_sd).then_inc(rms_ready, 1)

            def first_lo(i):
                dve.wait_ge(hi_ready, i + 1)
                nc.vector.tensor_tensor(w_lo[:, i, :], raw[:, i, :], w_hi[:, i, :].bitcast(F32),
                                        ALU.subtract).then_inc(lo_ready, 1)

            def scale_x(c):
                dve.wait_ge(x_landed[c], 16)
                scale_rows(c)

            dve.wait_ge(gain0_landed, 16)
            scale_x(0)
            first_lo(0)
            rows_lo(0, 0)
            first_lo(1)
            dve.wait_ge(gain_landed, 16)
            scale_x(1)
            first_lo(2)
            rows_lo(0, 1)
            scale_x(2)
            first_lo(3)

            def constants():
                dve.wait_ge(scaled_ready, N4)
                nc.vector.memset(glu[:, :, 0:PAD], 0.0)
                nc.vector.memset(v_band[0:64, 0, :], 0.0)
                dve.wait_ge(iota_ready, 2)
                link(nc.vector.scalar_tensor_tensor(
                    out=dist[:, :, :].rearrange("p t s -> p (t s)"), in0=dist_raw,
                    scalar=-1.0, in1=dist_raw, op0=ALU.mult, op1=ALU.max))
                link(nc.vector.memset(dist[0:CHUNK, 0, 0:CHUNK], 1e30))
                dve.wait_ge(params_landed, 10 * 16)
                nc.vector.tensor_copy(sink[:].rearrange("p (g b a) -> p g b a", a=2, b=2),
                                      sink_rows[:].rearrange("p (g a b) -> p g b a", a=2, b=2))

            def parameters():
                dve.wait_ge(aux_written[0], AUX0_PARAMS + 1)
                nc.vector.tensor_copy(dw_t[:], ps[:, 4, :].rearrange("p (m k) -> p m k", k=32)[:, :, 0:TAPS])
                link(nc.vector.tensor_copy(vecs[:], ps[:, 5, 0:NVEC]))
                nc.vector.tensor_scalar(q_gain[:], vecs[:, V_QG:V_QG + 1], HD ** -0.5, None, ALU.mult)
                nc.vector.tensor_copy(ffn_dw[:], ps[:, 5, P:P + 6 * FT].rearrange("p (k m) -> p k m", k=3)
                                      ).then_inc(aux_drained[0], 1)

            def rms(n):
                dve.wait_ge(ssq_ready, (n + 1) * TT * N4)
                link(nc.vector.tensor_reduce(ssq_all, ssq, AX_X, ALU.add))
                nc.vector.tensor_scalar(rms_ms, ssq_all, 1.0 / D, EPS, ALU.mult, ALU.add).then_inc(ms_ready, 1)

            def glu_product(j):
                left_psum(dve, Q_U + 1, j)
                nc.vector.tensor_tensor(stage2, stage1, stage3, ALU.mult).then_inc(glu_ready, 1)

            chunk(Q_U, {3: lambda: rows_lo(0, 2), 4: lambda: scale_x(3), 5: lambda: rows_lo(0, 3), 6: constants})
            rms(0)
            inverse(0)
            chunk(Q_U + 1, {1: parameters})
            FIRST_STEPS = {5: 5, 6: 5, 7: 4}
            chunk(Q_U + 2, {0: lambda: glu_product(0)}, conv_run(0, FIRST_STEPS, False))
            done = sum(FIRST_STEPS.values())
            for c in range(Q_U + 3, Q_Q0):
                chunk(c, {} if c % 2 else {0: lambda: glu_product(c // 2 - 1)}, conv_run(done, CONV_STEPS, False))
                done += per_chunk

            def head_rms(n_heads, n):
                w = n_heads * HD
                dve.wait_ge(hs_squared, n + 1)
                for t in range(TT):
                    last = nc.vector.tensor_reduce(
                        hs_sum[:, t * n_heads:(t + 1) * n_heads],
                        stage3[:, t, 0:w].rearrange("p (h d) -> p h d", d=HD), AX_X, ALU.add)
                link(last)
                nh = TT * n_heads
                if nh < 16:
                    link(nc.vector.memset(hs_sum[:, nh:16], 1.0))
                nc.vector.tensor_scalar(hs_ms, hs_sum, 1.0 / HD, EPS, ALU.mult, ALU.add).then_inc(hs_ms_ready, 1)

            def head_inverse(n):
                dve.wait_ge(hs_sd_ready, n + 1)
                link(nc.vector.reciprocal(hs_r, hs_sd))

            def heads_of(r, t, n_heads):
                return r[:, t * n_heads:(t + 1) * n_heads].unsqueeze(2).to_broadcast([P, n_heads, HD])

            def k_start():
                dve.wait_ge(consts_done, 1)
                left_psum(dve, Q_KV)
                dve.wait_ge(aux_drained[0], AUX0_GLU + N4)
                for t in range(TT):
                    nc.vector.tensor_copy(v_band[:, 2 * t + 1, :], stage1[:, t, KV_W:])
                head_rms(KV_HEADS, 0)

            def k_rows():
                head_inverse(0)
                for t in range(TT):
                    for dup in range(2):
                        dst = stage2[:, t, :].rearrange("p (g u d) -> p g u d", u=2, d=HD)[:, :, dup, :]
                        last = nc.vector.tensor_tensor(dst, stage1[:, t, 0:KV_W].rearrange("p (g d) -> p g d", d=HD),
                                                       heads_of(hs_r, t, KV_HEADS), ALU.mult)
                last.then_inc(k_ready, 1)

            chunk(Q_Q0, {0: k_start, 2: k_rows}, conv_run(done, CONV_STEPS, False))

            def q_start(j):
                left_psum(dve, Q_Q0, j)
                head_rms(GROUP, j + 1)

            def q_rows(j):
                head_inverse(j + 1)
                nc.vector.tensor_copy(v_head[:], v_band[:, :, ds(j * HD, HD)])
                nc.vector.tensor_copy(k_head[:], k_t[:, ds(j, 1), :].rearrange("p g t -> p (g t)"))
                for t in range(TT):
                    last = nc.vector.tensor_tensor(
                        stage2[:, t, :].rearrange("p (h d) -> p h d", d=HD),
                        stage1[:, t, :].rearrange("p (h d) -> p h d", d=HD), heads_of(hs_r, t, GROUP), ALU.mult)
                last.then_inc(qn_ready, 1)

            def maxima(j, e):
                b = e
                dve.wait_ge(aux_written[b], (AUX0_ATT + 1 + j * 3, AUX1_ATT + 2 + j * 4)[e])
                p = (prob0, prob1)[e]
                s = soft[:, e]
                for n in range(4):
                    last = nc.vector.scalar_tensor_tensor(
                        out=p[:, n * 256:(n + 1) * 256], in0=dist[:, :, :].rearrange("p t s -> p (t s)"),
                        scalar=neg_slope[:, ds(j * GROUP + 4 * e + n, 1)],
                        in1=aux(b).rearrange("p b n -> p (b n)")[:, n * 256:(n + 1) * 256],
                        op0=ALU.mult, op1=ALU.add)
                last.then_inc(aux_drained[b], 1)
                dve.wait_ge(aux_drained[b], (AUX0_ATT + 1 + j * 3, AUX1_ATT + 2 + j * 4)[e])
                link(nc.vector.tensor_reduce(s[:, 0, :], p.rearrange("p (n s) -> p n s", s=P), AX_X, ALU.max))
                sk = sink[:, ds(j * GROUP + 4 * e, 4)].unsqueeze(2).to_broadcast([P, 4, TT])
                m = s[:, 0, :].rearrange("p (n t) -> p n t", t=TT)
                link(nc.vector.tensor_tensor(m, m, sk, ALU.max))
                nc.vector.tensor_scalar(s[:, 1, :], s[:, 0, :], -1.0, None, ALU.mult)
                nc.vector.tensor_tensor(s[:, 2, :].rearrange("p (n t) -> p n t", t=TT), sk, m,
                                        ALU.subtract).then_inc(max_ready, 1)

            def probs(j, e):
                dve.wait_ge(exp_ready, j * 2 + e + 1)
                p = (prob0, prob1)[e].rearrange("p (n s) -> p n s", s=P)
                s = soft[:, e]
                link(nc.vector.tensor_tensor(s[:, 5, :], s[:, 3, :], s[:, 4, :], ALU.add))
                link(nc.vector.reciprocal(s[:, 0, :], s[:, 5, :]))
                nc.vector.tensor_tensor(p, p, s[:, 0, :].unsqueeze(2).to_broadcast([P, 8, P]),
                                        ALU.mult).then_inc(prob_ready, 1)

            def o_lo(j, e):
                dve.wait_ge(o_hi_ready, j * 2 + e + 1)
                at = ds(j * 4 + 2 * e, 2)
                nc.vector.tensor_tensor(B_lo[:, at, :], aux_tiles(1)[:, 2 * e:2 * e + 2, :], B_hi[:, at, :].bitcast(F32),
                                        ALU.subtract).then_inc(aux_drained[1], 1)

            def att_hooks(j):
                return ({0: lambda: q_start(j), 2: lambda: q_rows(j), 6: lambda: maxima(j, 0),
                         7: lambda: maxima(j, 1)},
                        {1: lambda: probs(j, 0), 3: lambda: probs(j, 1),
                         7: lambda: o_lo(j, 0)})

            def early_mean_out():
                dve.wait_ge(early_mean_written, 1)
                nc.vector.tensor_scalar(early_mean, ps[:, 7, 0:SEQ], KT / EARLY, None, ALU.mult
                                        ).then_inc(early_mean_ready, 1)
                dve.wait_ge(early_mean_ready, 1)

            def att_conv(m):
                return spread(m, 1, 2, {-1: 4, 2: 2, 3: 4, 4: 4, 5: 4}), spread(m, 1, 20, {3: 4, 4: 4, 5: 4})

            with links.loop(0, N4 - 1, 10) as j:
                first, second = att_hooks(j)
                conv_1, conv_2 = att_conv(j + 7)
                chunk(Q_ATT + j * 2, first, conv_1)
                chunk(Q_ATT + 1 + j * 2, second, conv_2)
                o_lo(j, 1)
            first, second = att_hooks(N4 - 1)
            conv_1, conv_2 = att_conv(LATE - 1)
            LATE_STEPS = {6: 6, 7: 6}
            chunk(Q_AP - 2, first, conv_1)
            chunk(Q_AP - 1, {**second, 4: early_mean_out}, {**conv_2, **conv_run(0, LATE_STEPS, True)})
            o_lo(N4 - 1, 1)

            def gate_attention(c, j, group):
                cols = ds(group * COLS, COLS)
                dve.wait_ge(piece_used, (c + 1) * PIECES + j * 16)
                nc.vector.tensor_tensor(gates_a[:, :, cols], gates_a[:, :, cols], acc(c % 2),
                                        ALU.mult).then_inc(evacuated[c % 2], 1)

            def centre_early(c):
                m0, m1 = LN_PARTS[c]
                y = glu[:, m0:m1, PAD:]
                nc.vector.tensor_tensor(y, y, early_mean.unsqueeze(1).to_broadcast([P, m1 - m0, SEQ]),
                                        ALU.subtract).then_inc(centred, 1)

            done = sum(LATE_STEPS.values())
            for c in range(Q_AP, Q_AP + 5):
                chunk(c, {Q_AP + 1: {5: lambda: centre_early(0)}, Q_AP + 4: {5: lambda: centre_early(1)}}.get(c, {}),
                      conv_run(done, CONV_STEPS, True))
                done += per_chunk
                if c % 2 == Q_AP % 2:
                    gate_attention(c, 0, (c - Q_AP) // 2)

            def ln_variance():
                dve.wait_ge(aux_written[0], AUX0_LN + 1)
                nc.vector.tensor_copy(rest_mean, ps[:, 4, 0:SEQ]).then_inc(aux_drained[0], 1)
                dve.wait_ge(aux_drained[0], AUX0_LN + 1)
                dve.wait_ge(aux_written[1], AUX1_LN + 1)
                link(nc.vector.tensor_tensor(mean_sq, rest_mean, rest_mean, ALU.mult))
                nc.vector.scalar_tensor_tensor(out=conv_var, in0=ps[:, 6, 0:SEQ], scalar=EPS, in1=mean_sq,
                                               op0=ALU.add, op1=ALU.subtract).then_inc(aux_drained[1], 1)

            def ln_inverse():
                dve.wait_ge(var_sd, 1)
                link(nc.vector.reciprocal(conv_r, conv_sd))

            def ln_scale(c):
                y = glu[:, 4 * c:4 * c + 4, PAD:]
                link(nc.vector.tensor_tensor(y, y, rest_mean.unsqueeze(1).to_broadcast([P, 4, SEQ]), ALU.subtract))
                nc.vector.tensor_tensor(y, y, conv_r.unsqueeze(1).to_broadcast([P, 4, SEQ]),
                                        ALU.mult).then_inc(ln_scaled, 1)

            def ln_lo(c):
                dve.wait_ge(conv_hi, c + 1)
                nc.vector.tensor_tensor(A_lo[:, 4 * c:4 * c + 4, :], glu[:, 4 * c:4 * c + 4, PAD:],
                                        A_hi[:, 4 * c:4 * c + 4, :].bitcast(F32), ALU.subtract).then_inc(conv_lo, 1)

            chunk(Q_AP + 5, {1: lambda: centre_early(2), 7: ln_variance},
                  conv_run(done, {-1: (KT - LATE) * STEPS - done}, True))
            chunk(Q_CP - 1, {1: ln_inverse, 2: lambda: ln_scale(0), 3: lambda: ln_scale(1), 5: lambda: ln_lo(0),
                             6: lambda: ln_scale(2), 7: lambda: ln_lo(1)})

            def mix_rows(c):
                q = Q_CP + c
                cols = slice(c * COLS, (c + 1) * COLS)
                dve.wait_ge(piece_used, (q + 1) * PIECES)
                left_psum(dve, Q_CP - 2)
                nc.vector.tensor_tensor(mix_n, gates_b[:, :, cols], acc(q % 2), ALU.mult).then_inc(evacuated[q % 2], 1)
                dve.wait_ge(evacuated[q % 2], q // 2 + 1)
                nc.vector.tensor_tensor(mix_n, mix_n, gates_a[:, :, cols], ALU.add).then_inc(mix_ready, 1)

            def mix_lo(c):
                dve.wait_ge(mix_hi, c + 1)
                nc.vector.tensor_tensor(B_lo[:, 4 * c:4 * c + 4, :], aux_tiles(c % 2),
                                        B_hi[:, 4 * c:4 * c + 4, :].bitcast(F32),
                                        ALU.subtract).then_inc(aux_drained[c % 2], 1)

            for c in range(N4):
                chunk(Q_CP + c, {4: lambda: mix_lo(c - 1)} if c else
                      {0: lambda: ln_scale(3), 2: lambda: ln_lo(2), 4: lambda: ln_lo(3),
                       6: lambda: gate_attention(Q_CP - 1, 0, N4 - 1)})
                mix_rows(c)

            def residual(c):
                q = Q_OUT + c
                cols = slice(c * COLS, (c + 1) * COLS)
                dve.wait_ge(piece_used, (q + 1) * PIECES)
                nc.vector.tensor_tensor(xres[:, :, cols], xres[:, :, cols], acc(q % 2),
                                        ALU.add).then_inc(evacuated[q % 2], 1)
                left_psum(dve, q)
                scale_rows(c)

            chunk(Q_OUT, {4: lambda: mix_lo(N4 - 1)})
            dve.wait_ge(x_reloaded, 16)
            dve.wait_ge(gain_landed, 32)
            residual(0)
            for c in range(1, N4):
                chunk(Q_OUT + c, {3: lambda: rows_lo(1, c - 1)})
                residual(c)

            def ffn_taps(b, uses, dst, col, k):
                if k == 2 and b is not None:
                    dve.wait_ge(aux_written[b], uses)
                tiles = last_val if b is None else aux_tiles(b)
                d = 2 - k
                for m in range(4):
                    w = ffn_dw[:, k, ds(col + m, 1)]
                    src = tiles[:, m, 0:SEQ - d]
                    if d == 0:
                        last = nc.vector.tensor_scalar(dst[:, m, :], src, w, None, ALU.mult)
                    else:
                        last = nc.vector.scalar_tensor_tensor(out=dst[:, m, d:], in0=src, scalar=w,
                                                              in1=dst[:, m, d:], op0=ALU.mult, op1=ALU.add)
                if k > 0 or b is None:
                    link(last)
                return last

            def conv_g(j, k):
                last = ffn_taps(0, AUX_UP + 1 + j, g_t, j * 4, k)
                if k == 0:
                    last.then_inc(aux_drained[0], 1)

            def conv_last_val(k):
                if k == 2:
                    dve.wait_ge(aux_drained[1], AUX_UP + UP_PAIRS)
                ffn_taps(None, None, val_t, (UP_PAIRS - 1) * 4 + FT, k)

            def conv_val(j, k):
                last = ffn_taps(1, AUX_UP + 1 + j, val_t, j * 4 + FT, k)
                if k == 0:
                    last.then_inc(aux_drained[1], 1)
                    dve.wait_ge(aux_drained[1], AUX_UP + 1 + j)

            def gated(j):
                dve.wait_ge(g_silu, j + 1)
                nc.vector.tensor_tensor(ff[:, ds(j * 4, 4), :], g_t, val_t, ALU.mult).then_inc(ff_ready, 1)

            def g_hooks(j):
                return {2: lambda: conv_g(j, 2), 3: lambda: conv_g(j, 1), 4: lambda: conv_g(j, 0)}

            def val_hooks(j):
                return {2: lambda: conv_val(j, 2), 3: lambda: conv_val(j, 1), 4: lambda: conv_val(j, 0),
                        5: lambda: gated(j)}

            chunk(Q_UP, {3: lambda: rows_lo(1, N4 - 1), 4: lambda: rms(1), 6: lambda: inverse(1)})
            with links.loop(0, UP_PAIRS - 1, 4) as j:
                chunk(Q_UP + 1 + j * 2, g_hooks(j))
                chunk(Q_UP + 2 + j * 2, val_hooks(j))

            def ff_lo(kt, s, n):
                dve.wait_ge(ff_hi_ready, n)
                nc.vector.tensor_tensor(B_lo[:, s:s + 1, :], ff[:, ds(kt, 1), :], B_hi[:, s:s + 1, :].bitcast(F32),
                                        ALU.subtract).then_inc(ff_lo_ready, 1)

            hooks = g_hooks(UP_PAIRS - 1)
            chunk(Q_DOWN - 1, {**hooks, 1: lambda: ff_lo(0, 0, 1), 5: lambda: ff_lo(1, 1, 2),
                               6: lambda: ff_lo(2, 2, 3), 7: lambda: ff_lo(3, 3, 4)})

            def down(it, hooks={}, last=False):
                for i in range(PIECE_LEAD if last else PIECES):
                    if i in hooks:
                        hooks[i]()
                    split_lo(Q_DOWN + it, i)
                    if i >= 4:
                        ff_lo(it * 4 + i, i - 4, it * 4 + i + 1)

            down(0, {3: lambda: conv_last_val(2), 4: lambda: conv_last_val(1), 5: lambda: conv_last_val(0),
                     6: lambda: gated(UP_PAIRS - 1)})
            with dve.Fori(1, N_DOWN - 1) as it:
                down(it)
            down(N_DOWN - 1, last=True)
            for n in range(N4):
                for t in range(TT):
                    done = Q_END * PIECES - (4 if n < 2 else 0)
                    if n % 2 and t == TT - 1:
                        dve.wait_ge(piece_used, done)
                    else:
                        dve.wait_ge(bank_done, n // 2 * 3 + n % 2 * TT + t + 1)
                    cols = slice(n * COLS, (n + 1) * COLS)
                    nc.vector.tensor_tensor(xres[:, t, cols], xres[:, t, cols], ps[:, DOWN_BANKS[n][t], :],
                                            ALU.add).then_inc(y_ready, 1)

        @block.tensor
        def _(pe):
            def piece(q, i, par, stat, first, last):
                s = i % PIECE_LEAD
                pe.wait_ge(lo_ready, q * PIECES + i + 1)
                for r in range(2):
                    k = 2 * i + r
                    hi, lo = w_hi[:, s, r * COLS:(r + 1) * COLS], w_lo[:, s, r * COLS:(r + 1) * COLS]
                    for t in range(TT):
                        o = ps[:, 2 * par + t, :]
                        a_hi, a_lo = (a[:, k, t * P:(t + 1) * P] for a in stat)
                        pe.matmul(o, a_hi, hi, start=(first and r == 0), stop=False)
                        pe.matmul(o, a_hi, lo, start=False, stop=False)
                        ins = pe.matmul(o, a_lo, hi, start=False, stop=(last and r == 1))
                ins.then_inc(piece_used, 1)

            def chunk(c, j, stat, hooks={}):
                if not (isinstance(j, int) and c + 2 * j < 2):
                    pe.wait_ge(evacuated[c % 2], j + c // 2)
                for i in range(PIECES):
                    if i in hooks:
                        hooks[i]()
                    piece(c + j * 2, i, c % 2, stat, i == 0, i == PIECES - 1)

            def aux_free(b, uses):
                if not (isinstance(uses, int) and uses == 0):
                    pe.wait_ge(aux_drained[b], uses)

            def transpose_rows(b, uses, src, m=4):
                aux_free(b, uses)
                for n in range(m):
                    for t in range(TT):
                        last = pe.transpose(aux_tiles(b)[:, n, t * P:(t + 1) * P], src[:, t, n * P:(n + 1) * P], ident[:])
                last.then_inc(aux_written[b], 1)

            def parameters():
                pe.wait_ge(params_landed, 10 * 16)
                aux_free(0, AUX0_PARAMS)
                for m in range(KT):
                    pe.transpose(ps[:, 4, m * 32:m * 32 + TAPS], rows_dw[:, m * P:(m + 1) * P], ident[0:TAPS, 0:TAPS])
                pe.transpose(ps[:, 5, 0:NVEC], rows_vec, ident[0:NVEC, 0:NVEC])
                for k in range(3):
                    last = pe.transpose(ps[:, 5, P + k * 2 * FT:P + (k + 1) * 2 * FT], rows_ffn[:, k, :],
                                        ident[0:2 * FT, 0:2 * FT])
                last.then_inc(aux_written[0], 1)

            def rows_in(n, base, c):
                pe.wait_ge(scaled_ready, 4 * n + c + 1)
                transpose_rows(c % 2, base + c // 2, scaled[c % 2])

            def rows_split(base, c):
                pe.wait_ge(aux_drained[c % 2], base + c // 2 + 1)

            A, B = (A_hi, A_lo), (B_hi, B_lo)
            pe.wait_ge(consts_ready, 1)
            rows_in(0, AUX_NORM1, 0)

            def glu_in(j):
                pe.wait_ge(glu_ready, j + 1)
                transpose_rows(0, j + AUX0_GLU, stage2)

            chunk(Q_U, 0, A, {0: lambda: rows_split(AUX_NORM1, 0), 1: lambda: rows_in(0, AUX_NORM1, 1),
                              2: lambda: rows_split(AUX_NORM1, 1), 3: lambda: rows_in(0, AUX_NORM1, 2),
                              4: lambda: rows_split(AUX_NORM1, 2), 5: lambda: rows_in(0, AUX_NORM1, 3),
                              6: lambda: rows_split(AUX_NORM1, 3),
                              7: parameters})
            chunk(Q_U + 1, 0, A)
            chunk(Q_U + 2, 0, A, {3: lambda: glu_in(0)})
            with pe.Fori(1, N4 - 1) as j:
                chunk(Q_U + 1, j, A)
                chunk(Q_U + 2, j, A, {3: lambda: glu_in(j)})
            chunk(Q_KV - 1, 0, A)
            chunk(Q_KV, 0, A, {3: lambda: glu_in(N4 - 1)})

            def k_in():
                pe.wait_ge(k_ready, 1)
                aux_free(1, AUX1_KV)
                for g in range(KV_HEADS):
                    for t in range(TT):
                        last = pe.transpose(aux_tiles(1)[:, g, t * P:(t + 1) * P], stage2[:, t, g * P:(g + 1) * P],
                                            ident[:])
                last.then_inc(aux_written[1], 1)

            chunk(Q_Q0, 0, A, {5: k_in})

            def q_in(j):
                pe.wait_ge(qn_ready, j + 1)
                transpose_rows(1, j * 4 + AUX1_ATT, stage2)

            def scores(j, e):
                if e == 0:
                    pe.wait_ge(aux_drained[1], j * 4 + AUX1_ATT + 1)
                aux_free(e, (j * 3 + AUX0_ATT, j * 4 + AUX1_ATT + 1)[e])
                pe.transpose(ps[:, 4 + 2 * e, 0:P], ident[:], ident[:])
                for n in range(4):
                    pair, half = 2 * e + n // 2, 64 * (n % 2)
                    for c in range(NCHUNK):
                        rows = slice(64 * (c % 2), 64 * (c % 2) + 64)
                        cols = (n // 2) * 256 + (c // 2) * P
                        last = pe.matmul(ps[rows, 4 + 2 * e + n % 2, cols:cols + P],
                                         q_t[half:half + 64, pair, c * CHUNK:(c + 1) * CHUNK],
                                         k_head[half:half + 64, c * CHUNK:c * CHUNK + P], start=True, stop=True)
                last.then_inc(aux_written[e], 1)

            def probs_in(j, e):
                pe.wait_ge(prob_ready, j * 2 + e + 1)
                aux_free(0, j * 3 + AUX0_ATT + 1 + e)
                p = (prob0, prob1)[e]
                for n in range(8):
                    last = pe.transpose(aux(0).rearrange("p b n -> p (b n)")[:, n * P:(n + 1) * P],
                                        p[:, n * P:(n + 1) * P], ident[:])
                last.then_inc(aux_written[0], 1)

            def values(j, e):
                pe.wait_ge(aux_drained[0], j * 3 + AUX0_ATT + 2 + e)
                aux_free(1, j * 4 + AUX1_ATT + 2)
                if isinstance(j, int):
                    pe.wait_ge(early_mean_ready, 1)
                for n in range(4):
                    half, at = 64 * (n % 2), score_place(n) * 256
                    for c in range(NCHUNK):
                        cols = (n // 2) * SEQ + c * CHUNK
                        last = pe.matmul(ps[half:half + 64, 6 + e, cols:cols + CHUNK], v_head[:, c, :],
                                         prob_t[:, at + c * CHUNK:at + (c + 1) * CHUNK],
                                         start=True, stop=True)
                last.then_inc(aux_written[1], 1)

            def att_hooks(j):
                return ({5: lambda: q_in(j), 6: lambda: (scores(j, 0), scores(j, 1))},
                        {4: lambda: probs_in(j, 0), 6: lambda: (values(j, 0), probs_in(j, 1)),
                         7: lambda: values(j, 1)})

            def channel_mean(dst, src, first, last):
                return pe.matmul(dst, mean_of[:], src, start=first, stop=last)

            def early_tiles_mean():
                pe.wait_ge(consts_done, 1)
                aux_free(1, AUX1_LN - 2)
                pe.wait_ge(conv_tap, EARLY * EARLY_STEPS)
                for m in range(EARLY):
                    last = channel_mean(ps[:, 7, 0:SEQ], glu[:, m, PAD:], m == 0, m == EARLY - 1)
                last.then_inc(early_mean_written, 1)

            with pe.Fori(0, N4 - 1) as j:
                first, second = att_hooks(j)
                chunk(Q_ATT, j, A, first)
                chunk(Q_ATT + 1, j, A, second)
            first, second = att_hooks(N4 - 1)
            chunk(Q_AP - 2, 0, A, first)
            chunk(Q_AP - 1, 0, A, {**second, 3: early_tiles_mean})

            def some():
                pe.wait_ge(aux_drained[1], AUX1_LN - 4)

            def rest():
                pe.wait_ge(aux_drained[1], AUX1_LN)


            def late_tiles_mean():
                aux_free(0, AUX0_LN)
                pe.wait_ge(centred, 3)
                pe.wait_ge(conv_tap, ALL_CONV_STEPS)
                for m in range(EARLY, KT):
                    last = channel_mean(ps[:, 4, 0:SEQ], glu[:, m, PAD:], m == EARLY, m == KT - 1)
                last.then_inc(aux_written[0], 1)

            def mean_squares(c):
                if c == 0:
                    aux_free(1, AUX1_LN)
                pe.wait_ge(squared, c + 1)
                for m in range(*LN_PARTS[c]):
                    last = channel_mean(ps[:, 6, 0:SEQ], squares[:, m, :], m == 0, m == KT - 1)
                if c == 3:
                    last.then_inc(aux_written[1], 1)

            chunk(Q_AP, 0, B, {0: some, 6: rest})
            chunk(Q_AP + 1, 0, A)
            chunk(Q_AP + 2, 0, B, {3: lambda: mean_squares(0)})
            chunk(Q_AP + 3, 0, A)
            chunk(Q_AP + 4, 0, B)
            chunk(Q_AP + 5, 0, A, {3: lambda: mean_squares(1), 5: late_tiles_mean,
                                   6: lambda: (mean_squares(2), mean_squares(3))})
            chunk(Q_CP - 1, 0, B)

            def mix_in(c):
                pe.wait_ge(mix_ready, c + 1)
                transpose_rows(c % 2, AUX_MIX + c // 2, mix_n)

            for c in range(N4):
                hooks = {2: lambda: mix_in(c - 1)} if c else {2 * g: (lambda g=g: pe.wait_ge(conv_lo, g + 1))
                                                             for g in range(4)}
                chunk(Q_CP + c, 0, A, hooks)

            def mixed(c):
                pe.wait_ge(aux_drained[c % 2], AUX_MIX + c // 2 + 1)

            mixed(0), mixed(1), mixed(2)
            chunk(Q_OUT, 0, B, {2: lambda: mix_in(N4 - 1), 6: lambda: mixed(N4 - 1)})
            for c in range(1, N4):
                chunk(Q_OUT + c, 0, B, {2: lambda: rows_in(1, AUX_NORM2, c - 1)})

            def up_in(b, uses, c, j=0):
                left_psum(pe, c, j)
                transpose_rows(b, uses, up_n)

            for c in range(3):
                rows_split(AUX_NORM2, c)
            chunk(Q_UP, 0, A, {2: lambda: rows_in(1, AUX_NORM2, 3), 6: lambda: rows_split(AUX_NORM2, 3)})
            with pe.Fori(0, UP_PAIRS - 1) as j:
                chunk(Q_UP + 1, j, A, {1: lambda: up_in(0, j + AUX_UP, Q_UP, j)})
                chunk(Q_UP + 2, j, A, {1: lambda: up_in(1, j + AUX_UP, Q_UP + 1, j)})
            chunk(Q_DOWN - 1, 0, A, {1: lambda: up_in(0, AUX_UP + UP_PAIRS - 1, Q_DOWN - 2)})

            left_psum(pe, Q_DOWN - 2)
            aux_free(0, AUX_UP + UP_PAIRS)

            def last_val():
                up_in(1, AUX_UP + UP_PAIRS - 1, Q_DOWN - 1)

            def right_banks():
                left_psum(pe, Q_DOWN - 1)
                aux_free(1, AUX_UP + UP_PAIRS)

            def down(it, hooks={}, first=False, last=False):
                for i in range(PIECES):
                    if i in hooks:
                        hooks[i]()
                    s = i % PIECE_LEAD
                    pe.wait_ge(lo_ready, (Q_DOWN + it) * PIECES + i + 1)
                    kt, half = i % 4, i // 4
                    if half == 0:
                        pe.wait_ge(ff_lo_ready, it * 4 + kt + 1)
                    starts, stops = first and kt == 0, last and kt == 3
                    for r in range(2):
                        n = 2 * half + r
                        hi, lo = w_hi[:, s, r * COLS:(r + 1) * COLS], w_lo[:, s, r * COLS:(r + 1) * COLS]
                        for t in range(TT):
                            o = ps[:, DOWN_BANKS[n][t], :]
                            a_hi, a_lo = (a[:, kt, t * P:(t + 1) * P] for a in B)
                            pe.matmul(o, a_hi, hi, start=starts, stop=False)
                            pe.matmul(o, a_hi, lo, start=False, stop=False)
                            ins = pe.matmul(o, a_lo, hi, start=False, stop=stops)
                            if stops and not (r == 1 and t == TT - 1):
                                ins.then_inc(bank_done, 1)
                    ins.then_inc(piece_used, 1)

            down(0, {1: last_val, 4: right_banks}, first=True)
            with pe.Fori(1, N_DOWN - 1) as it:
                down(it)
            down(N_DOWN - 1, last=True)


_INS = ['x', 'norm_mix_g', 'w_in', 'q_norm_g', 'k_norm_g', 'sinks', 'w_attn_proj', 'conv_dw_w', 'conv_dw_b',
        'conv_ln_g', 'conv_ln_b', 'w_conv_proj', 'w_out', 'norm_ffn_g', 'w_up', 'ffn_dw_w', 'w_down']
_OUTS = [((1, 256, 2048), 'float32')]


def kernel(**inputs):
    import numpy as _np
    import concourse.bacc as _bacc
    from concourse import mybir as _mybir
    from concourse.bass_utils import run_bass_kernel_spmd as _run

    nc = _bacc.Bacc("TRN2", target_bir_lowering=False, num_devices=1)
    arrays, args = {}, []
    for name in _INS:
        a = _np.ascontiguousarray(inputs[name])
        arrays[f"in_{name}_dram"] = a
        args.append(nc.dram_tensor(f"in_{name}_dram", a.shape, _mybir.dt.from_np(a.dtype), kind="ExternalInput").ap())
    for i, (shape, dtype) in enumerate(_OUTS):
        dt = _mybir.dt.from_np(_np.dtype(dtype))
        args.append(nc.dram_tensor(f"out_{i}_dram", shape, dt, kind="ExternalOutput").ap())
    trunk(nc, *args)
    r = _run(nc, [arrays], core_ids=[0])
    got = tuple(r.results[0][f"out_{i}_dram"] for i in range(len(_OUTS)))
    return got[0]
```
